# Optimizing a Trainium2 kernel written in Bass

```python
import jax, jax.numpy as jnp
from jax import lax
import numpy as np

D_MODEL = 1024
BATCH = 1
SEQ = 512
DEPTH = 1

MLA_HEADS = 4
MLA_Q_RANK = 384
MLA_KV_RANK = 256
MLA_NOPE = 128
MLA_ROPE = 64
MLA_V = 128
ROPE_THETA = 10000.0
ATTN_BLOCK = 128

GLA_HEADS = 4
GLA_DK = 64
GLA_DV = 128
GLA_GATE_RANK = 16
GLA_GATE_NORM = 16.0
GLA_CHUNK = 64

MIX_WIDTH = MLA_HEADS * MLA_V + GLA_HEADS * GLA_DV

IN_SIZES = (MLA_Q_RANK, MLA_KV_RANK, MLA_ROPE,
            GLA_HEADS * GLA_DK, GLA_HEADS * GLA_DK, GLA_HEADS * GLA_DV,
            GLA_GATE_RANK, GLA_GATE_RANK, GLA_HEADS * GLA_DV)
IN_WIDTH = sum(IN_SIZES)

PEER_HEADS = 8
PEER_NKEYS = 128
PEER_EXPERTS = PEER_NKEYS * PEER_NKEYS
PEER_DKEY = 256
PEER_TOPK = 16
PEER_BLOCK = 128

NORM_EPS = 1e-6

kernel_name = 'hymba_mla_gla_peer_adaln_encoder'

def rmsnorm(x, g):
    xf = x.astype(jnp.float32)
    y = xf * lax.rsqrt(jnp.mean(xf * xf, axis=-1, keepdims=True) + NORM_EPS)
    return (y * g.astype(jnp.float32)).astype(x.dtype)

def rope(x, positions):
    d = x.shape[-1]
    half = d // 2
    inv = ROPE_THETA ** (-jnp.arange(half, dtype=jnp.float32) / half)
    ang = positions.astype(jnp.float32)[..., None] * inv
    ang = ang.reshape(ang.shape[:2] + (1,) * (x.ndim - 3) + (half,))
    cos, sin = jnp.cos(ang), jnp.sin(ang)
    xf = x.astype(jnp.float32)
    x1, x2 = xf[..., :half], xf[..., half:]
    return jnp.concatenate([x1 * cos - x2 * sin, x2 * cos + x1 * sin], axis=-1).astype(x.dtype)

def block_attention(q, k, v):
    B, S, H, dq = q.shape
    nb = S // ATTN_BLOCK
    scale = dq ** -0.5
    qb = q.reshape(B, nb, ATTN_BLOCK, H, dq).transpose(1, 0, 2, 3, 4)

    def one_block(qblk):
        s = jnp.einsum('bqhd,bkhd->bhqk', qblk, k).astype(jnp.float32) * scale
        p = jax.nn.softmax(s, axis=-1).astype(v.dtype)
        return jnp.einsum('bhqk,bkhv->bqhv', p, v)

    out = lax.map(one_block, qb)
    return out.transpose(1, 0, 2, 3, 4).reshape(B, S, H, v.shape[-1])

def gla_chunked(q, k, v, log_a):
    B, S, H, dk = q.shape
    dv = v.shape[-1]
    C = GLA_CHUNK
    n = S // C

    def blocks(t):
        return t.astype(jnp.float32).reshape(B, n, C, H, t.shape[-1]).transpose(0, 3, 1, 2, 4)

    qc, kc, vc, gc = blocks(q), blocks(k), blocks(v), blocks(log_a)
    b = jnp.cumsum(gc, axis=3)
    b_last = b[:, :, :, -1:, :]
    q_dec = qc * jnp.exp(b)
    k_inv = kc * jnp.exp(-b)
    lower = jnp.tril(jnp.ones((C, C), dtype=bool))
    att = jnp.where(lower, jnp.einsum('bhnid,bhnjd->bhnij', q_dec, k_inv), 0.0)
    o_intra = jnp.einsum('bhnij,bhnjv->bhniv', att, vc)
    d_state = jnp.einsum('bhnjd,bhnjv->bhndv', kc * jnp.exp(b_last - b), vc)
    chunk_decay = jnp.exp(b_last[:, :, :, 0, :])

    def step(state, inp):
        dec, ds = inp
        return dec[..., None] * state + ds, state

    _, s_prev = lax.scan(step, jnp.zeros((B, H, dk, dv), jnp.float32),
                         (jnp.moveaxis(chunk_decay, 2, 0), jnp.moveaxis(d_state, 2, 0)))
    s_prev = jnp.moveaxis(s_prev, 0, 2)
    o = o_intra + jnp.einsum('bhnid,bhndv->bhniv', q_dec, s_prev)
    return o.transpose(0, 2, 3, 1, 4).reshape(B, S, H, dv)

def token_mixer(h, positions, w_in, g_q_latent, w_q_up, g_kv_latent, w_kv_up,
                w_gate_fwd, b_gate_fwd, w_gate_bwd, b_gate_bwd, g_gla_norm, w_out):
    B, S, _ = h.shape
    proj = h @ w_in
    offs = np.cumsum(IN_SIZES)[:-1].tolist()
    (cq, ckv, k_rope_raw, qg, kg, vg,
     gl_fwd, gl_bwd, r) = jnp.split(proj, offs, axis=-1)

    qa = (rmsnorm(cq, g_q_latent) @ w_q_up).reshape(B, S, MLA_HEADS, MLA_NOPE + MLA_ROPE)
    q_nope, q_rope = qa[..., :MLA_NOPE], rope(qa[..., MLA_NOPE:], positions)
    kv = (rmsnorm(ckv, g_kv_latent) @ w_kv_up).reshape(B, S, MLA_HEADS, MLA_NOPE + MLA_V)
    k_nope, v_mla = kv[..., :MLA_NOPE], kv[..., MLA_NOPE:]
    k_rope = rope(k_rope_raw, positions)
    q_mla = jnp.concatenate([q_nope, q_rope], axis=-1)
    k_mla = jnp.concatenate(
        [k_nope, jnp.broadcast_to(k_rope[:, :, None, :], (B, S, MLA_HEADS, MLA_ROPE))], axis=-1)
    o_mla = block_attention(q_mla, k_mla, v_mla).reshape(B, S, MLA_HEADS * MLA_V)

    qg = qg.reshape(B, S, GLA_HEADS, GLA_DK) * (GLA_DK ** -0.5)
    kg = kg.reshape(B, S, GLA_HEADS, GLA_DK)
    vg = vg.reshape(B, S, GLA_HEADS, GLA_DV)
    la_fwd = (jax.nn.log_sigmoid((gl_fwd @ w_gate_fwd + b_gate_fwd).astype(jnp.float32))
              / GLA_GATE_NORM).reshape(B, S, GLA_HEADS, GLA_DK)
    la_bwd = (jax.nn.log_sigmoid((gl_bwd @ w_gate_bwd + b_gate_bwd).astype(jnp.float32))
              / GLA_GATE_NORM).reshape(B, S, GLA_HEADS, GLA_DK)
    o_f = gla_chunked(qg, kg, vg, la_fwd)
    flip = lambda t: jnp.flip(t, axis=1)
    o_b = flip(gla_chunked(flip(qg), flip(kg), flip(vg), flip(la_bwd)))
    o_g = rmsnorm((o_f + o_b).astype(h.dtype), g_gla_norm)
    o_gla = (o_g * jax.nn.silu(r.reshape(B, S, GLA_HEADS, GLA_DV))).reshape(B, S, GLA_HEADS * GLA_DV)

    return jnp.concatenate([o_mla, o_gla], axis=-1) @ w_out

def peer(h, w_peer_q, sub_keys_1, sub_keys_2, expert_u, expert_v):
    B, S, D = h.shape
    half = PEER_DKEY // 2
    tokens = h.reshape(-1, PEER_BLOCK, D)

    def one_block(xb):
        P = xb.shape[0]
        qry = (xb @ w_peer_q).reshape(P, PEER_HEADS, PEER_DKEY)
        s1 = jnp.einsum('phd,nd->phn', qry[..., :half], sub_keys_1).astype(jnp.float32)
        s2 = jnp.einsum('phd,nd->phn', qry[..., half:], sub_keys_2).astype(jnp.float32)
        v1, i1 = lax.top_k(s1, PEER_TOPK)
        v2, i2 = lax.top_k(s2, PEER_TOPK)
        cand_s = (v1[..., :, None] + v2[..., None, :]).reshape(P, PEER_HEADS, PEER_TOPK * PEER_TOPK)
        cand_i = (i1[..., :, None] * PEER_NKEYS + i2[..., None, :]).reshape(P, PEER_HEADS, PEER_TOPK * PEER_TOPK)
        top_s, pos = lax.top_k(cand_s, PEER_TOPK)
        eidx = jnp.take_along_axis(cand_i, pos, axis=-1)
        gates = jax.nn.softmax(top_s, axis=-1)
        u = expert_u[eidx]
        a = jnp.einsum('phkd,pd->phk', u, xb).astype(jnp.float32)
        w = (gates * jax.nn.gelu(a, approximate=False)).astype(xb.dtype)
        return jnp.einsum('phk,phkd->pd', w, expert_v[eidx])

    return lax.map(one_block, tokens).reshape(B, S, D)

def setup_inputs(seed: int = 0) -> dict:
    key = jax.random.key(seed)
    ks = jax.random.split(key, 32)
    L, D = DEPTH, D_MODEL
    nrm = lambda k, shape, fan: jax.random.normal(k, shape, jnp.float32) * (fan ** -0.5)
    gain = lambda k, shape: 1.0 + 0.05 * jax.random.normal(k, shape, jnp.float32)
    x = jax.random.normal(ks[0], (BATCH, SEQ, D), jnp.float32)
    c = jax.random.normal(ks[1], (BATCH, D), jnp.float32)
    offsets = jax.random.randint(ks[2], (BATCH, 1), 0, 1024, dtype=jnp.int32)
    positions = jnp.arange(SEQ, dtype=jnp.int32)[None, :] + offsets
    return {
        'x': x,
        'c': c,
        'positions': positions,
        'w_ada': 0.5 * nrm(ks[3], (L, D, 6 * D), D),
        'b_ada': 0.01 * jax.random.normal(ks[4], (L, 6 * D), jnp.float32),
        'g_pre_mix': gain(ks[5], (L, D)),
        'g_post_mix': gain(ks[6], (L, D)),
        'w_in': nrm(ks[7], (L, D, IN_WIDTH), D),
        'g_q_latent': gain(ks[8], (L, MLA_Q_RANK)),
        'w_q_up': nrm(ks[9], (L, MLA_Q_RANK, MLA_HEADS * (MLA_NOPE + MLA_ROPE)), MLA_Q_RANK),
        'g_kv_latent': gain(ks[10], (L, MLA_KV_RANK)),
        'w_kv_up': nrm(ks[11], (L, MLA_KV_RANK, MLA_HEADS * (MLA_NOPE + MLA_V)), MLA_KV_RANK),
        'w_gate_fwd': nrm(ks[12], (L, GLA_GATE_RANK, GLA_HEADS * GLA_DK), GLA_GATE_RANK),
        'b_gate_fwd': 0.1 * jax.random.normal(ks[13], (L, GLA_HEADS * GLA_DK), jnp.float32),
        'w_gate_bwd': nrm(ks[14], (L, GLA_GATE_RANK, GLA_HEADS * GLA_DK), GLA_GATE_RANK),
        'b_gate_bwd': 0.1 * jax.random.normal(ks[15], (L, GLA_HEADS * GLA_DK), jnp.float32),
        'g_gla_norm': gain(ks[16], (L, GLA_DV)),
        'w_out': nrm(ks[17], (L, MIX_WIDTH, D), MIX_WIDTH),
        'g_pre_ffn': gain(ks[18], (L, D)),
        'g_post_ffn': gain(ks[19], (L, D)),
        'w_peer_q': nrm(ks[20], (L, D, PEER_HEADS * PEER_DKEY), D),
        'sub_keys_1': nrm(ks[21], (L, PEER_NKEYS, PEER_DKEY // 2), PEER_DKEY // 2),
        'sub_keys_2': nrm(ks[22], (L, PEER_NKEYS, PEER_DKEY // 2), PEER_DKEY // 2),
        'expert_u': nrm(ks[23], (L, PEER_EXPERTS, D), D),
        'expert_v': nrm(ks[24], (L, PEER_EXPERTS, D), D),
    }

def reference(x, c, positions, w_ada, b_ada, g_pre_mix, g_post_mix, w_in, g_q_latent, w_q_up,
              g_kv_latent, w_kv_up, w_gate_fwd, b_gate_fwd, w_gate_bwd, b_gate_bwd, g_gla_norm,
              w_out, g_pre_ffn, g_post_ffn, w_peer_q, sub_keys_1, sub_keys_2, expert_u, expert_v):
    c_act = jax.nn.silu(c)
    for l in range(DEPTH):
        mod = (c_act @ w_ada[l] + b_ada[l])[:, None, :]
        sh1, sc1, gt1, sh2, sc2, gt2 = jnp.split(mod, 6, axis=-1)
        h = rmsnorm(x, g_pre_mix[l]) * (1.0 + sc1) + sh1
        y = token_mixer(h, positions, w_in[l], g_q_latent[l], w_q_up[l], g_kv_latent[l], w_kv_up[l],
                        w_gate_fwd[l], b_gate_fwd[l], w_gate_bwd[l], b_gate_bwd[l], g_gla_norm[l], w_out[l])
        x = x + gt1 * rmsnorm(y, g_post_mix[l])
        h = rmsnorm(x, g_pre_ffn[l]) * (1.0 + sc2) + sh2
        y = peer(h, w_peer_q[l], sub_keys_1[l], sub_keys_2[l], expert_u[l], expert_v[l])
        x = x + gt2 * rmsnorm(y, g_post_ffn[l])
    return x


_drawn_inputs = setup_inputs


def setup_inputs(seed=0):
    import zlib

    import numpy as np

    out = dict(_drawn_inputs(seed))
    spreads = {}
    factors = {'g_q_latent': 4.312, 'g_post_ffn': 3.942}
    for name, (base, spread) in spreads.items():
        noise = np.random.default_rng([zlib.crc32(name.encode()), seed]).standard_normal(out[name].shape)
        drawn = base * np.exp(spread * noise) if base else spread * noise
        out[name] = __import__('jax').numpy.asarray(drawn.astype(out[name].dtype))
    for name, factor in factors.items():
        out[name] = (out[name] * factor).astype(out[name].dtype)
    return out
```

```python
import concourse.bass as bass
from concourse import mybir
from contextlib import ExitStack

P = 128
D, SEQ = 1024, 512
KD, NT = D // P, SEQ // P
Q_RANK, KV_RANK = 384, 256
MLA_H, NOPE, ROPE, DV = 4, 128, 64, 128
GLA_H, DK, CHUNK = 4, 64, 64
NCH = SEQ // CHUNK
GATE_RANK, GATE_NORM = 16, 16.0
PH, NKEYS, DKEY, TOPK = 8, 128, 256, 16
NEXP = NKEYS * NKEYS
EPS = 1e-6
THETA = 10000.0
TWO_PI = 6.283185307179586
PI_A = 6.28125
PI_B = 0.001934051513671875
PI_C = TWO_PI - PI_A - PI_B
HALF_PI = 1.5707963267948966
PI_MAX = 3.1415925
ROUND = 12582912.0
NEG = -3.0e38

N_MOD = 6 * KD
COL_B = 0
COL_GPM, COL_GQM, COL_GPF, COL_GQF = N_MOD, N_MOD + 8, N_MOD + 16, N_MOD + 24
COL_GQL = N_MOD + 32
COL_GKVL = COL_GQL + 3
COL_BG = COL_GKVL + 2
COL_GGLA = COL_BG + 4
COL_INV, COL_SIGN, COL_EPS = COL_GGLA + 1, COL_GGLA + 2, COL_GGLA + 3
NCOLS = COL_EPS + 1
GT1, SC2, SH2, GT2 = (k * KD for k in range(2, 6))
MOD_ORDER = (1, 0, 2, 4, 3, 5)

K_ID, K_ONES, K_TRI, K_SCAN, K_IOTA = 0, P, 2 * P, 3 * P, 3 * P + SEQ
NCONST = K_IOTA + TOPK

IN_TILES = 14
IN_CHUNKS = IN_TILES + 4
CQ, CKV, KRG, QG, KG, RG = 0, 3, 5, 6, 8, 10

NB = 8
GROUP = NT * TOPK

O_COLS = 0
O_CONST = O_COLS + NCOLS + (NCOLS & 1)
O_KEYS = O_CONST + NCONST
O_X = 1280
O_SMALL = O_X + NT * D
O_UP = 5600
O_W = O_UP + 5120
O_ADA = O_W + 8 * 1024
O_H1T = O_ADA + 8192
O_LAT = O_H1T + KD * SEQ
O_KROPE = O_LAT + 5 * SEQ
O_QG = O_KROPE + SEQ
O_KG = O_QG + 2 * SEQ
O_R = O_KG + 2 * SEQ
O_VG = O_R + 4 * SEQ
O_GL = O_VG + 4 * SEQ
O_E = O_GL + SEQ
O_TAB = O_E + 7 * 1024
O_TMP = O_TAB + 2 * SEQ
O_END = O_TMP + 2 * SEQ
O_PERM = O_END + 3 * SEQ
SBUF_WORDS = 53200
O_YACC = O_UP
O_DIAG = O_YACC + NT * D
O_FOUT = O_W
O_BC = O_H1T
O_SLOTS = [(O_ADA if b < 4 else O_LAT) + (b % 4) * 2 * D for b in range(NB)]
O_JUNK = O_LAT + 4 * 2 * D
O_H2 = O_GL
O_H2T = O_H2 + NT * D
O_TOPK = O_H2T + KD * SEQ
O_QT = 50128
O_WQ = SBUF_WORDS - 2048


def build(nc, x_d, c_d, pos_d, ada_d, cols_d, const_d, keys_d, win_d, perm_d, wqup_d, wkvup_d, wgate_d,
          wout_d, wpq_d, uv_d, out_d):
    f32, u32, i32 = mybir.dt.float32, mybir.dt.uint32, mybir.dt.int32
    ACT, ALU, AX = mybir.ActivationFunctionType, mybir.AluOpType, mybir.AxisListType
    ctx = ExitStack()
    with ctx:
        A = ctx.enter_context(nc.sbuf_tensor("arena", [P, SBUF_WORDS], f32))
        ps = ctx.enter_context(nc.psum_tensor("ps", [P, 8, 512], f32))

        def sem(name):
            return ctx.enter_context(nc.semaphore(name))

        def at(off, *shape):
            n = 1
            for s in shape:
                n *= s
            v = A[:, off:off + n]
            if len(shape) == 2:
                return v.rearrange("p (a b) -> p a b", a=shape[0])
            if len(shape) == 3:
                return v.rearrange("p (a b c) -> p a b c", a=shape[0], b=shape[1])
            return v

        cols = at(O_COLS, NCOLS)
        const = at(O_CONST, NCONST)
        ident, ones = const[:, K_ID:K_ID + P], const[:, K_ONES:K_ONES + P]
        tri = const[:, K_TRI:K_TRI + 2 * CHUNK].rearrange("p (d i) -> p d i", d=2)
        scan_keep = const[:, K_SCAN:K_SCAN + SEQ]
        iota = const[:, K_IOTA:K_IOTA + TOPK]
        keys = at(O_KEYS, 2, NKEYS)
        X = at(O_X, NT, D)
        small = at(O_SMALL, 224)
        mod = small[:, 0:N_MOD]
        ss, sd, rstd = small[:, 48:52], small[:, 52:56], small[:, 56:60]
        nmax, rsum, rinv = small[:, 64:80], small[:, 80:96], small[:, 96:112]
        edge = small[:, 112:144].rearrange("p (i c) -> p i c", i=4)
        ssb, sdb, rstdb = small[:, 144:148], small[:, 148:152], small[:, 152:156]
        smax = small[:, 160:176]
        eps = cols[:, COL_EPS:COL_EPS + 1]

        cact = at(O_E, D)
        craw = at(O_TAB, D)
        xn = at(O_E + D, NT, D)
        ada = at(O_ADA, 4, 2, D)
        wring = at(O_W, 8, 1024)
        wqup, wkvup = at(O_UP, 3, 6, P), at(O_UP + 3072, 2, 1024)
        h1T = at(O_H1T, KD, SEQ)
        latT = at(O_LAT, 5, SEQ)
        krope = at(O_KROPE, SEQ)
        qgT, kgT = at(O_QG, 2, SEQ), at(O_KG, 2, SEQ)
        rT, vg = at(O_R, 4, SEQ), at(O_VG, NT, SEQ)
        krgT = at(O_GL, SEQ)
        perm = at(O_PERM, 3 * P)
        swap_q, dup_k, swap_k = (perm[:, k * P:(k + 1) * P] for k in range(3))
        qn, qr, kn, vm = (at(O_E, 4, SEQ), at(O_E + 2048, 2, SEQ), at(O_E + 3072, 4, SEQ),
                          at(O_E + 5120, NT, SEQ))
        cos_t, sin_t = at(O_TAB, SEQ), at(O_TAB + SEQ, SEQ)
        tmp = at(O_TMP, 2, SEQ)
        latsq = at(O_E + D, 5, SEQ)
        wgate = at(O_END, 2, 2, P)
        turned = at(O_END + 512, 2, SEQ)
        pos_i, ang, turn = (at(O_VG + k * SEQ, SEQ) for k in range(3))
        prob, probT = at(O_ADA, 4, SEQ), at(O_ADA + 2048, NT, SEQ)
        mixT = at(O_UP, 8, SEQ)
        gate = at(O_W + 2048, 4, SEQ)
        soft = at(O_W + 4096, 4, SEQ)
        qdec = at(O_H1T, 2, GLA_H, SEQ)
        kinv = at(O_ADA + 4096, 4, SEQ)
        kdecT = at(O_ADA + 6144, 4, SEQ)
        gtmp = at(O_END, 3, SEQ)
        kdec = at(O_ADA, 4, 2, 512)
        state = at(O_E, 4, 7 * 256)
        att = [at(O_QG, GLA_H, 512), at(O_LAT, GLA_H, 512)]
        gsq = at(O_TMP, 2, SEQ)
        grs = at(O_END, 2, SEQ)
        diag8 = at(O_E, 8, 512)
        bcast = at(O_BC, 4, D)
        wout = at(O_W, KD, D)
        h2, h2T = at(O_H2, NT, D), at(O_H2T, KD, SEQ)
        junk = at(O_JUNK, 1, D)
        yacc, ring = at(O_YACC, NT, D), [at(o, 2 * D) for o in O_SLOTS]
        wpq, qT = at(O_WQ, KD, DKEY), at(O_QT, 2, SEQ)
        fout = at(O_FOUT, NT, D)
        o = [O_TOPK]

        def small_buf(n):
            o[0] += n
            assert o[0] <= O_QT
            return A[:, o[0] - n:o[0]]

        v12 = small_buf(32).rearrange("p (a b) -> p a b", a=2)
        i12 = small_buf(32).bitcast(u32).rearrange("p (a b) -> p a b", a=2)
        i12f = small_buf(32).rearrange("p (a b) -> p a b", a=2)
        srest = small_buf(256).rearrange("p (a b) -> p a b", a=2)
        cand, crest = small_buf(256), small_buf(256)
        tops = small_buf(NT * TOPK).rearrange("p (a b) -> p a b", a=NT)
        posn = small_buf(16).bitcast(u32)
        pab = small_buf(32).bitcast(u32).rearrange("p (a b) -> p a b", a=2)
        pabf = small_buf(32).rearrange("p (a b) -> p a b", a=2)
        sel = small_buf(32).rearrange("p (a b) -> p a b", a=2)
        eidx = small_buf(NT * TOPK).bitcast(u32).rearrange("p (a b) -> p a b", a=NT)
        etop = small_buf(NT * TOPK).rearrange("p (a b) -> p a b", a=NT)
        gates = small_buf(NT * TOPK).rearrange("p (a b) -> p a b", a=NT)
        adot = small_buf(NT * TOPK).rearrange("p (a b) -> p a b", a=NT)
        agelu = small_buf(NT * TOPK).rearrange("p (a b) -> p a b", a=NT)
        wexp = small_buf(NT * TOPK).rearrange("p (a b) -> p a b", a=NT)
        nmx, tsum, tinv = small_buf(NT), small_buf(NT), small_buf(NT)
        dg, onehot = at(O_DIAG, 4, P), at(O_DIAG + 4 * P, 2, TOPK, TOPK)

        c_in, small_in, x_in, up_in = sem("c_in"), sem("small_in"), [sem(f"x_in{t}") for t in range(NT)], sem("up_in")
        ada_in, ada_used = [sem(f"ada_in{k}") for k in range(4)], sem("ada_used")
        win_in = [sem(f"win_in{k}") for k in range(8)]
        wout_in, wpq_in = sem("wout_in"), sem("wpq_in")
        dve_step, act_step, pool_step = sem("dve_step"), sem("act_step"), sem("pool_step")
        c_act, ms_ready, xn_ready = sem("c_act"), sem("ms_ready"), sem("xn_ready")
        xT_done, mod1_ready, mods_ready = sem("xT_done"), sem("mod1_ready"), sem("mods_ready")
        h1_ready, pos_in = sem("h1_ready"), sem("pos_in")
        kr_done, kr_read = sem("kr_done"), sem("kr_read")
        angles, tables = sem("angles"), sem("tables")
        proj_act = sem("proj_act")
        lat_done, sq_ready, ss_done, ss_read = (sem("lat_done"), sem("sq_ready"), sem("ss_done"),
                                                sem("ss_read"))
        lat_ready, z_done, z_read, gate_exp = (sem("lat_ready"), sem("z_done"), sem("z_read"),
                                               sem("gate_exp"))
        vg_done, vg_evac = sem("vg_done"), sem("vg_evac")
        upq_done, up_act, up_dve = sem("upq_done"), sem("up_act"), sem("up_dve")
        s_done, max_ready, exp_done, prob_ready = (sem("s_done"), sem("max_ready"), sem("exp_done"),
                                                   sem("prob_ready"))
        pt_done, pt_evac, o_done, o_evac = sem("pt_done"), sem("pt_evac"), sem("o_done"), sem("o_evac")
        zeros_ready, sums_ready, decay_ready = (sem("zeros_ready"), sem("sums_ready"),
                                                sem("decay_ready"))
        qdec_ready, kdec_ready = sem("qdec_ready"), sem("kdec_ready")
        decay_dve = sem("decay_dve")
        kd_done, kd_act, kd_dve = sem("kd_done"), sem("kd_act"), sem("kd_dve")
        ds_done, state_ready = sem("ds_done"), sem("state_ready")
        zeros2, att_done, att_ready = sem("zeros2"), sem("att_done"), sem("att_ready")
        og_done, gsq_ready, gss_done, gsd_ready, mix_ready = (
            sem("og_done"), sem("gsq_ready"), sem("gss_done"), sem("gsd_ready"), sem("mix_ready"))
        diag_cols, bc_done, bc_evac = sem("diag_cols"), sem("bc_done"), sem("bc_evac")
        y_done, ssy_ready, x1_ready, ssx_ready = (sem("y_done"), sem("ssy_ready"), sem("x1_ready"),
                                                  sem("ssx_ready"))
        h2_ready, h2T_done, h2T_evac = sem("h2_ready"), sem("h2T_done"), sem("h2T_evac")
        query_done, query_evac, scores_done = sem("query_done"), sem("query_evac"), sem("scores_done")
        topk_step, topk_done, topk_exp, gates_ready = (sem("topk_step"), sem("topk_done"),
                                                       sem("topk_exp"), sem("gates_ready"))
        rows_in = [sem(f"rows_in{b}") for b in range(NB)]
        dots_done, gelu_done, weight_done, diag_ready = (sem("dots_done"), sem("gelu_done"),
                                                         sem("weight_done"), sem("diag_ready"))
        slot_summed, y_taken, y_zero = sem("slot_summed"), sem("y_taken"), sem("y_zero")
        first_query, first_evac = sem("first_query"), sem("first_evac")
        rope_ready, tinv_done = sem("rope_ready"), sem("tinv_done")
        ssf_ready, out_ready, out_written = sem("ssf_ready"), sem("out_ready"), sem("out_written")

        def linker(eng, own):
            count = {}

            def tell(ins, s=own):
                count[s.name] = count.get(s.name, 0) + 1
                ins.then_inc(s, 1)

            def link(ins, s=own):
                tell(ins, s)
                eng.wait_ge(s, count[s.name])

            return tell, link

        def hold(eng, s, value):
            eng.wait_ge(s, value)
            if not isinstance(value, int):
                eng.nop(nofuse=True)

        def wait_unit_evacuated(pe, u):
            if u in (6, 7):
                pe.wait_ge(up_dve, 2 * (u - 5))
            else:
                pe.wait_ge(up_act, u + 1 if u < 6 else u - 1)

        block = ctx.enter_context(nc.Block())

        @block.sync
        def _(sp):
            def load_x(t):
                sp.dma_start(X[:, t], x_d[t * P:(t + 1) * P, :]).then_inc(x_in[t], 16)

            def load_win(n):
                if n >= 8:
                    sp.wait_ge(lat_done, 1 if n < 11 else n - 7)
                sp.dma_start(wring[:, n % 8], win_d[:, n, :]).then_inc(win_in[n % 8], 16)

            sp.dma_start(craw, c_d.partition_broadcast(P)).then_inc(c_in, 16)
            load_x(0)
            load_x(1)
            sp.dma_start(const, const_d).then_inc(small_in, 16)
            sp.dma_start(cols, cols_d).then_inc(small_in, 16)
            load_x(2)
            load_x(3)
            load_win(0)
            for n in range(1, 8):
                sp.wait_ge(ada_used, min(4 * n - 2, 16))
                load_win(n)
            sp.dma_start(pos_i.bitcast(i32), pos_d.partition_broadcast(P)).then_inc(pos_in, 16)
            sp.dma_start(keys, keys_d).then_inc(up_in, 16)
            sp.dma_start(perm, perm_d).then_inc(up_in, 16)
            sp.dma_start(wgate[64:96], wgate_d).then_inc(up_in, 16)
            sp.dma_start(wqup, wqup_d).then_inc(up_in, 16)
            sp.dma_start(wkvup, wkvup_d).then_inc(up_in, 16)
            for n in range(8, IN_CHUNKS):
                load_win(n)
            sp.wait_ge(vg_done, NT)
            sp.wait_ge(kdec_ready, 8)
            sp.wait_ge(qdec_ready, 8)
            sp.dma_start(wout, wout_d).then_inc(wout_in, 16)
            sp.wait_ge(mix_ready, GLA_H)
            sp.dma_start(wpq, wpq_d[0]).then_inc(wpq_in, 16)
            with sp.Fori(1, PH) as h:
                sp.wait_ge(query_done, h * 2)
                sp.dma_start(wpq, wpq_d[bass.ds(h, 1)].rearrange("o p k n -> p (o k) n")).then_inc(wpq_in, 16)
            for t in range(NT):
                sp.wait_ge(out_ready, t + 1)
                sp.dma_start(out_d[t * P:(t + 1) * P, :], fout[:, t]).then_inc(out_written, 16)
            sp.wait_ge(out_written, 16 * NT)

        @block.gpsimd
        def _(pool):
            g = nc.gpsimd
            _, link = linker(pool, pool_step)
            for n in range(24):
                if n >= 4:
                    pool.wait_ge(ada_used, 2 * (n - 3))
                g.dma_start(ada[:, n % 4], ada_d[:, n, :, :]).then_inc(ada_in[n % 4], 16)
            pool.wait_ge(vg_done, NT)
            for d in range(2):
                for h in range(GLA_H):
                    r0 = 64 * (1 - h % 2)
                    link(g.memset(qdec[r0:r0 + 64, d, h], 0.0), zeros_ready)
            for i in range(4):
                pool.wait_ge(decay_ready, 2 * i + 1)
                link(g.tensor_tensor(kinv[:, i], kgT[:, i % 2], gtmp[:, 1], ALU.mult), kdec_ready)
                pool.wait_ge(decay_ready, 2 * i + 2)
                link(g.tensor_tensor(kdecT[:, i], kgT[:, i % 2], gtmp[:, 2], ALU.mult), kdec_ready)
            pool.wait_ge(pt_evac, 4 * MLA_H)
            pool.wait_ge(o_done, MLA_H)
            for i in range(4):
                link(g.memset(kdec[64:P, i, 0], 0.0), zeros2)
                link(g.memset(kdec[0:64, i, 1], 0.0), zeros2)
            pool.wait_ge(kdec_ready, 8)
            pool.wait_ge(qdec_ready, 8)
            for d in range(2):
                for h in range(GLA_H):
                    v = att[d][:, h].rearrange("p (t c) -> p t c", t=NT)
                    link(g.memset(v[0:64, :, 64:P], 0.0), zeros2)
                    link(g.memset(v[64:P, :, 0:64], 0.0), zeros2)
            def fetch(h):
                for t in range(NT):
                    hold(pool, topk_done, 4 * h + t + 1)
                    for s in range(TOPK):
                        n = h * GROUP + t * TOPK + s
                        b = (t * TOPK + s) % NB
                        if isinstance(h, int) and n == NB:
                            pool.wait_ge(y_done, NT)
                            link(g.memset(yacc[:, NT - 1], 0.0), y_zero)
                        if not isinstance(h, int) or n >= NB:
                            hold(pool, slot_summed, n - NB + 1)
                        g.indirect_dma_start(
                            ring[b], None, uv_d,
                            bass.IndirectOffsetOnAxis(ap=eidx[:, t, s:s + 1], axis=0),
                        ).then_inc(rows_in[b], 16)

            fetch(0)
            with pool.Fori(1, PH) as h:
                fetch(h)

        @block.scalar
        def _(act):
            a = nc.scalar
            tell, link = linker(act, act_step)
            act.wait_ge(c_in, 16)
            link(a.activation(cact, craw, ACT.Silu), c_act)
            for t in range(NT):
                act.wait_ge(x_in[t], 16)
                if t == 0:
                    act.wait_ge(small_in, 32)
                link(a.activation(xn[:, t], X[:, t], ACT.Square, accum_out=ss[:, t:t + 1]))
                link(a.activation(sd[:, t:t + 1], ss[:, t:t + 1], ACT.Sqrt, scale=1.0 / D, bias=eps), ms_ready)
            for d in range(KD):
                act.wait_ge(xT_done, d + 1)
                act.wait_ge(mod1_ready, d + 1)
                tell(a.activation(h1T[:, d], ps[:, 4 + d % 4], ACT.Identity, scale=mod[:, 2 * d:2 * d + 1],
                                  bias=mod[:, 2 * d + 1:2 * d + 2]), h1_ready)

            def proj_copy(i, out, **kw):
                act.wait_ge(lat_done, i + 1)
                tell(a.activation(out, ps[:, i % 4], kw.pop("func", ACT.Copy), **kw), proj_act)

            for i in range(5):
                act.wait_ge(lat_done, i + 1)
                tell(a.activation(latsq[:, i], ps[:, i % 4], ACT.Square), sq_ready)
                proj_copy(i, latT[:, i], scale=cols[:, COL_GQL + i:COL_GQL + i + 1])
                if i == 3:
                    act.wait_ge(angles, 2)
                    tell(a.activation(cos_t, turn, ACT.Sin), tables)
                    tell(a.activation(sin_t, ang, ACT.Sin, scale=cols[:, COL_SIGN:COL_SIGN + 1]), tables)
            proj_copy(KRG, krgT)
            for j in range(2):
                proj_copy(QG + j, qgT[:, j], scale=DK ** -0.5)
            for j, rank in enumerate((Q_RANK, KV_RANK)):
                act.wait_ge(ss_done, j + 1)
                tell(a.activation(tmp[:, j], ps[:, 4 + j], ACT.Sqrt, scale=1.0 / rank, bias=eps), ss_read)
            for j in range(2):
                proj_copy(KG + j, kgT[:, j])
            for j in range(4):
                proj_copy(RG + j, rT[:, j], func=ACT.Silu)
            for i in range(4):
                act.wait_ge(z_read, i + 1)
                link(a.activation(soft[:, i], gate[:, i], ACT.Abs))
                link(a.activation(soft[:, i], soft[:, i], ACT.Exp, scale=-1.0))
                tell(a.activation(soft[:, i], soft[:, i], ACT.Ln, bias=1.0), gate_exp)
            for t in range(NT):
                act.wait_ge(vg_done, t + 1)
                tell(a.activation(vg[:, t], ps[:, 4 + t], ACT.Copy), vg_evac)
            act.wait_ge(mods_ready, 1)
            act.wait_ge(ss_read, 2)
            act.wait_ge(lat_ready, 5)
            for u in (0, 1, 2, 3, 4, 5, 8, 9, 10, 11, 12, 13, 14, 15):
                act.wait_ge(upq_done, u + 1)
                dst = qn[:, u] if u < 4 else tmp[:, u - 4] if u < 6 else kn[:, u - 8] if u < 12 else vm[:, u - 12]
                tell(a.activation(dst, ps[:, u % 4], ACT.Copy), up_act)

            def decays(i):
                act.wait_ge(sums_ready, 2 * i + 1)
                if i >= 1:
                    act.wait_ge(qdec_ready, 2 * i)
                    act.wait_ge(kdec_ready, 2 * i)
                tell(a.activation(gtmp[:, 0], gate[:, i], ACT.Exp, scale=1.0 / GATE_NORM), decay_dve)
                tell(a.activation(gtmp[:, 1], gate[:, i], ACT.Exp, scale=-1.0 / GATE_NORM), decay_ready)
                act.wait_ge(sums_ready, 2 * i + 2)
                tell(a.activation(gtmp[:, 2], tmp[:, i % 2], ACT.Exp, scale=1.0 / GATE_NORM), decay_ready)
                link(a.activation(edge[:, i], gate[:, i][:, (CHUNK - 1 if i < 2 else 0)::CHUNK], ACT.Exp,
                                  scale=1.0 / GATE_NORM), decay_dve)

            scale = (NOPE + ROPE) ** -0.5
            for n in range(16 + 2):
                if n < 16:
                    act.wait_ge(max_ready, n + 1)
                    if n >= 4:
                        act.wait_ge(pt_done, n - 3)
                    tell(a.activation(prob[:, n % 4], ps[:, n % 4], ACT.Exp, scale=scale,
                                      bias=nmax[:, n:n + 1], accum_out=rsum[:, n:n + 1]), exp_done)
                m = n - 2
                if m >= 0:
                    act.wait_ge(pt_done, m + 1)
                    if m % 4 == 0 and m:
                        act.wait_ge(o_done, m // 4)
                    tell(a.activation(probT[:, :, (m % 4) * P:(m % 4 + 1) * P],
                                      ps[:, 4 + m % 2].rearrange("p (k q) -> p k q", k=NT), ACT.Copy),
                         pt_evac)
                    if m % 4 == 0 and m:
                        act.wait_ge(o_done, m // 4)
                        tell(a.activation(mixT[:, m // 4 - 1], ps[:, 6], ACT.Copy), o_evac)
                if n % 4 == 3:
                    decays(n // 4)
            act.wait_ge(o_done, 4)
            tell(a.activation(mixT[:, 3], ps[:, 6], ACT.Copy), o_evac)

            act.wait_ge(zeros2, 8)
            for i in range(4):
                act.wait_ge(kd_done, i + 1)
                tell(a.activation(kdec[0:64, i, 0], ps[0:64, i], ACT.Copy), kd_act)
            for h in range(GLA_H):
                act.wait_ge(og_done, h + 1)
                if h >= 2:
                    act.wait_ge(gss_done, h - 1)
                tell(a.activation(gsq[:, h % 2], ps[:, h], ACT.Square), gsq_ready)
                act.wait_ge(gss_done, h + 1)
                if h >= 2:
                    act.wait_ge(mix_ready, h - 1)
                tell(a.activation(grs[:, h % 2], ps[:, 4 + h], ACT.Sqrt, scale=1.0 / DV, bias=eps), gsd_ready)
            for u in range(8):
                act.wait_ge(bc_done, u + 1)
                tell(a.activation(bcast[:, u // 2, (u % 2) * 512:(u % 2 + 1) * 512], ps[:, 4 + u % 4],
                                  ACT.Copy), bc_evac)
            def square_y(t):
                act.wait_ge(y_done, t + 1)
                b0 = 2 * (t % 2)
                link(a.activation(junk[:, 0].rearrange("p (a b) -> p a b", a=2), ps[:, b0:b0 + 2], ACT.Square,
                                  accum_out=ss[:, t:t + 1]))
                link(a.activation(sd[:, t:t + 1], ss[:, t:t + 1], ACT.Sqrt, scale=1.0 / D, bias=eps),
                     ssy_ready)

            def square_x(t):
                act.wait_ge(x1_ready, 2 * t + 2)
                link(a.activation(junk[:, 0], X[:, t], ACT.Square, accum_out=ssb[:, t:t + 1]))
                link(a.activation(sdb[:, t:t + 1], ssb[:, t:t + 1], ACT.Sqrt, scale=1.0 / D, bias=eps),
                     ssx_ready)

            def copy_h2T(t):
                act.wait_ge(h2T_done, t + 1)
                b0 = 2 if t == 3 else 4
                for j in range(2):
                    tell(a.activation(h2T[:, 4 * j:4 * j + 4, t * P:(t + 1) * P],
                                      ps[:, b0 + j].rearrange("p (d q) -> p d q", d=4), ACT.Copy), h2T_evac)

            def copy_first_query(t):
                act.wait_ge(first_query, t + 1)
                for half in range(2):
                    tell(a.activation(qT[:, half, t * P:(t + 1) * P], ps[:, 4 + half, t * P:(t + 1) * P], ACT.Copy),
                         first_evac)

            def copy_query(h, half):
                act.wait_ge(query_done, 2 * h + half + 1)
                if not isinstance(h, int) or h > 0:
                    act.wait_ge(scores_done, 4 * h)
                a.activation(qT[:, half], ps[:, 4 + half], ACT.Copy).then_inc(query_evac, 1)

            def exp_top(h, t):
                act.wait_ge(topk_done, 4 * h + t + 1)
                a.activation(etop[:, t], tops[:, t], ACT.Exp, bias=nmx[:, t:t + 1],
                             accum_out=tsum[:, t:t + 1]).then_inc(topk_exp, 1)

            def pair(h, t, q):
                n = h * GROUP + t * TOPK + 2 * q
                k = slice(2 * q, 2 * q + 2)
                act.wait_ge(dots_done, n + 2)
                a.activation(agelu[:, t, k], adot[:, t, k], ACT.Gelu).then_inc(gelu_done, 1)
                if q == 0:
                    act.wait_ge(gates_ready, 4 * h + t + 1)
                act.wait_ge(gelu_done, h * (GROUP // 2) + t * (TOPK // 2) + q + 1)
                for s in (2 * q, 2 * q + 1):
                    a.activation(wexp[:, t, s:s + 1], agelu[:, t, s:s + 1], ACT.Copy,
                                 scale=gates[:, t, s:s + 1]).then_inc(weight_done, 1)
                for s in (2 * q, 2 * q + 1):
                    m = h * GROUP + t * TOPK + s
                    act.wait_ge(weight_done, m + 1)
                    if not isinstance(h, int) or m >= 4:
                        act.wait_ge(slot_summed, m - 3)
                    a.activation(dg[:, s % 4], ident, ACT.Copy,
                                 scale=wexp[:, t, s:s + 1]).then_inc(diag_ready, 1)

            def weigh(h, more):
                for t in range(NT):
                    for q in range(TOPK // 2):
                        first = isinstance(h, int) and h == 0 and t == 0
                        if first and q == 2:
                            square_y(3)
                        if first and q == 4:
                            last_tiles()
                        pair(h, t, q)
                        if q == (7 if first else 3) and more and t < 2:
                            copy_query(h + 1, t)
                        if q == (7 if first else 3):
                            if more or t < 3:
                                exp_top(h if t < 3 else h + 1, (t + 1) % NT)
                        if not more and t > 0 and q == 4:
                            square_sums(t - 1)

            def last_tiles():
                square_x(3)
                copy_h2T(2)
                copy_h2T(3)
                for half in range(2):
                    act.wait_ge(query_done, half + 1)
                    a.activation(qT[:, half, 2 * P:], ps[:, 4 + half, 2 * P:], ACT.Copy).then_inc(query_evac, 1)

            def square_sums(t):
                act.wait_ge(y_taken, NT * (PH - 1) + t + 1)
                link(a.activation(junk[:, 0], yacc[:, t], ACT.Square, accum_out=ss[:, t:t + 1]))
                link(a.activation(sd[:, t:t + 1], ss[:, t:t + 1], ACT.Sqrt, scale=1.0 / D, bias=eps),
                     ssf_ready)

            square_y(0)
            square_x(0)
            square_y(1)
            copy_h2T(0)
            square_x(1)
            copy_first_query(0)
            exp_top(0, 0)
            square_y(2)
            copy_h2T(1)
            square_x(2)
            copy_first_query(1)
            weigh(0, True)
            with act.Fori(1, PH - 1) as h:
                weigh(h, True)
            weigh(PH - 1, False)
            square_sums(3)

        @block.tensor
        def _(pe):
            mm = nc.tensor.matmul
            pe.wait_ge(small_in, 32)
            for t in range(NT):
                pe.wait_ge(xn_ready, t + 1)
                for d in range(4):
                    last = nc.tensor.transpose(ps[:, 4 + d, t * P:(t + 1) * P], xn[:, t, d * P:(d + 1) * P], ident)
                    if t == NT - 1:
                        last.then_inc(xT_done, 1)
            for k in range(KD):
                pe.wait_ge(h1_ready, k + 1)
                if k < 4:
                    for t in range(NT):
                        last = nc.tensor.transpose(ps[:, 4 + k, t * P:(t + 1) * P],
                                                   xn[:, t, (k + 4) * P:(k + 5) * P], ident)
                    last.then_inc(xT_done, 1)
                pe.wait_ge(win_in[k // 2], 16)
                w = wring[:, k // 2].rearrange("p (k m) -> p k m", k=2)
                for i in range(4):
                    last = mm(ps[:, i], w[:, k % 2, i * P:(i + 1) * P], h1T[:, k], start=(k == 0),
                              stop=(k == KD - 1), skip_group_check=True)
                    if k == KD - 1:
                        last.then_inc(lat_done, 1)

            def proj_tile(i):
                pe.wait_ge(win_in[i % 8], 16 * (i // 8 + 1))
                pe.wait_ge(proj_act, i - 3)
                w = wring[:, i % 8].rearrange("p (k m) -> p k m", k=KD)
                for k in range(KD):
                    last = mm(ps[:, i % 4], w[:, k], h1T[:, k], start=(k == 0), stop=(k == KD - 1))
                last.then_inc(lat_done, 1)

            proj_tile(4)
            proj_tile(5)
            for j, (k0, k1) in enumerate(((0, 3), (3, 5))):
                pe.wait_ge(sq_ready, k1)
                for k in range(k0, k1):
                    last = mm(ps[:, 4 + j], ones, latsq[:, k], start=(k == k0), stop=(k == k1 - 1))
                last.then_inc(ss_done, 1)
            proj_tile(6)
            pe.wait_ge(up_in, 80)
            pe.wait_ge(proj_act, KRG + 1)
            for j, m in enumerate((dup_k, swap_k)):
                mm(ps[:, 6 + j], m[0:ROPE], krgT[0:ROPE], start=True, stop=True).then_inc(kr_done, 1)
            for i in range(7, IN_TILES):
                proj_tile(i)
            pe.wait_ge(ss_read, 2)
            pe.wait_ge(kr_read, 2)
            for i in range(4):
                mm(ps[:, 4 + i], wgate[64:96, i // 2, i % 2], krgT[64:96], start=True, stop=True).then_inc(z_done, 1)
            pe.wait_ge(z_read, 4)
            for j in range(4):
                i = IN_TILES + j
                pe.wait_ge(win_in[i % 8], 16 * (i // 8 + 1))
                w = wring[:, i % 8].rearrange("p (k m) -> p k m", k=2)
                for t in range(NT):
                    for kk in range(2):
                        k = 2 * j + kk
                        last = mm(ps[:, 4 + t], h1T[:, k, t * P:(t + 1) * P], w[:, kk], start=(k == 0),
                                  stop=(k == KD - 1), skip_group_check=True)
                    if j == 3:
                        last.then_inc(vg_done, 1)
            for u in range(16):
                if u == 0:
                    pe.wait_ge(lat_ready, 3)
                if u == 8:
                    pe.wait_ge(lat_ready, 5)
                if u < 4:
                    pe.wait_ge(proj_act, IN_TILES - 1 - (IN_TILES - 1 - u) % 4 + 1)
                else:
                    wait_unit_evacuated(pe, u - 4)
                if 6 <= u < 8:
                    wait_unit_evacuated(pe, u - 2)
                    last = mm(ps[:, u % 4], swap_q, tmp[:, u - 6], start=True, stop=True)
                elif u < 6:
                    for k in range(3):
                        last = mm(ps[:, u % 4], wqup[:, k, u], latT[:, k], start=(k == 0), stop=(k == 2))
                elif u < 12:
                    for k in range(2):
                        last = mm(ps[:, u % 4], wkvup[:, k, (u - 8) * P:(u - 7) * P], latT[:, 3 + k],
                                  start=(k == 0), stop=(k == 1))
                else:
                    for k in range(2):
                        last = mm(ps[:, u % 4], latT[:, 3 + k, (u - 12) * P:(u - 11) * P], wkvup[:, k, 512:1024],
                                  start=(k == 0), stop=(k == 1))
                last.then_inc(upq_done, 1)

            def scores(n):
                h, q = n // 4, n % 4
                r = 64 * (h % 2)
                if n < 4:
                    wait_unit_evacuated(pe, 12 + n)
                else:
                    pe.wait_ge(exp_done, n - 3)
                mm(ps[:, n % 4], qn[:, h, q * P:(q + 1) * P], kn[:, h], start=True, stop=False)
                mm(ps[:, n % 4], qr[r:r + 64, h // 2, q * P:(q + 1) * P], krope[r:r + 64],
                   start=False, stop=True).then_inc(s_done, 1)

            def values(h):
                pe.wait_ge(pt_evac, 4 * h + 4)
                if h:
                    pe.wait_ge(o_evac, h)
                for k in range(NT):
                    last = mm(ps[:, 6], vm[:, k, h * P:(h + 1) * P], probT[:, k], start=(k == 0), stop=(k == 3))
                last.then_inc(o_done, 1)

            pe.wait_ge(up_act, 14)
            pe.wait_ge(rope_ready, 3)
            pe.wait_ge(vg_evac, NT)
            for n in range(3):
                scores(n)
            for n in range(16):
                pe.wait_ge(prob_ready, n + 1)
                if n >= 2:
                    pe.wait_ge(pt_evac, n - 1)
                for k in range(NT):
                    last = nc.tensor.transpose(ps[:, 4 + n % 2, k * P:(k + 1) * P],
                                               prob[:, n % 4, k * P:(k + 1) * P], ident)
                last.then_inc(pt_done, 1)
                if n + 3 < 16:
                    scores(n + 3)
                if n % 4 == 0 and n:
                    values(n // 4 - 1)
            values(3)

            pe.wait_ge(kdec_ready, 8)
            pe.wait_ge(exp_done, 16)
            for i in range(4):
                for t in range(NT):
                    last = nc.tensor.transpose(ps[:, i, t * P:(t + 1) * P], kdecT[:, i, t * P:(t + 1) * P], ident)
                last.then_inc(kd_done, 1)
            for i in range(4):
                d, p = i // 2, i % 2
                if i == 0:
                    pe.wait_ge(zeros2, 8)
                    pe.wait_ge(kd_act, 4)
                    pe.wait_ge(kd_dve, 4)
                    pe.wait_ge(o_evac, 4)
                else:
                    if i >= 2:
                        pe.wait_ge(state_ready, i - 1)
                b0 = 4 if i % 2 == 0 else 0
                for c in range(7):
                    cc = c if d == 0 else 7 - c
                    last = mm(ps[:, b0 + c // 2, (c % 2) * 256:(c % 2 + 1) * 256],
                              kdec[:, i, cc % 2, (cc // 2) * P:(cc // 2 + 1) * P],
                              vg[:, cc // 2, p * 256:(p + 1) * 256], start=True, stop=True)
                last.then_inc(ds_done, 1)
            pe.wait_ge(state_ready, 3)
            pe.wait_ge(zeros_ready, 8)
            pe.wait_ge(qdec_ready, 8)
            for d in range(2):
                for h in range(GLA_H):
                    i = d * 2 + h // 2
                    n = d * GLA_H + h
                    for t in range(NT):
                        for par in range(2):
                            k0 = t * P + par * 64
                            last = mm(ps[par * 64:par * 64 + 64, 4 + n // 2,
                                         (n % 2) * 256 + t * 64:(n % 2) * 256 + t * 64 + 64],
                                      kinv[:, i, k0:k0 + 64], qdec[:, d, h, k0:k0 + 64], start=True, stop=True)
                    last.then_inc(att_done, 1)
            pe.wait_ge(state_ready, 4)
            pe.wait_ge(zeros2, 24)
            pe.wait_ge(att_ready, 16)
            for h in range(GLA_H):
                p = h // 2
                for t in range(NT):
                    todo = []
                    for d in range(2):
                        todo.append((0, P, vg[:, t, h * P:(h + 1) * P], att[d][:, h, t * P:(t + 1) * P]))
                        for par in range(2):
                            c = 2 * t + par
                            k = c if d == 0 else 7 - c
                            if k == 0:
                                continue
                            st = state[:, d * 2 + p, (k - 1) * 256 + (h % 2) * P:(k - 1) * 256 + (h % 2 + 1) * P]
                            todo.append((par * 64, 64, st, qdec[:, d, h, c * 64:c * 64 + 64]))
                    for j, (o0, n, lhs, rhs) in enumerate(todo):
                        last = mm(ps[:, h, t * P + o0:t * P + o0 + n], lhs, rhs, start=(j == 0),
                                  stop=(j == len(todo) - 1), skip_group_check=True)
                last.then_inc(og_done, 1)
            for h in range(GLA_H):
                pe.wait_ge(gsq_ready, h + 1)
                mm(ps[:, 4 + h], ones, gsq[:, h % 2], start=True, stop=True).then_inc(gss_done, 1)
            for u in range(8):
                pe.wait_ge(diag_cols, u + 1)
                pe.wait_ge(gsd_ready, u % 4 + 1) if u < 4 else pe.wait_ge(bc_evac, u - 3)
                mm(ps[:, 4 + u % 4], ones, diag8[:, u], start=True, stop=True).then_inc(bc_done, 1)
            pe.wait_ge(wout_in, 16)
            pe.wait_ge(mix_ready, GLA_H)
            pe.wait_ge(bc_evac, 8)

            def project_out(t):
                b0 = 2 * (t % 2)
                if t >= 2:
                    pe.wait_ge(x1_ready, 2 * (t - 2) + 1)
                for half in range(2):
                    for k in range(KD):
                        last = mm(ps[:, b0 + half], mixT[:, k, t * P:(t + 1) * P],
                                  wout[:, k, half * 512:(half + 1) * 512], start=(k == 0), stop=(k == KD - 1))
                last.then_inc(y_done, 1)

            def transpose_h2(t):
                pe.wait_ge(h2_ready, t + 1)
                if t > 0:
                    pe.wait_ge(first_evac, 2 * min(t, 2))
                b0 = 2 if t == 3 else 4
                for d in range(KD):
                    last = nc.tensor.transpose(ps[:, b0 + d // 4, (d % 4) * P:(d % 4 + 1) * P],
                                               h2[:, t, d * P:(d + 1) * P], ident)
                last.then_inc(h2T_done, 1)

            def first_head(t0, t1):
                pe.wait_ge(h2T_evac, 2 * t1)
                for half in range(2):
                    for k in range(KD):
                        last = mm(ps[:, 4 + half, t0 * P:t1 * P], wpq[:, k, half * P:(half + 1) * P],
                                  h2T[:, k, t0 * P:t1 * P], start=(k == 0), stop=(k == KD - 1))
                    if t0 == 2:
                        last.then_inc(query_done, 1)
                if t0 < 2:
                    last.then_inc(first_query, 1)
                    pe.wait_ge(first_evac, 2 * t1)
                    if t0 == 1:
                        pe.wait_ge(topk_done, 1)
                    tile_scores(t0)
                else:
                    pe.wait_ge(query_evac, 2)
                    tile_scores(2)
                    tile_scores(3)

            def tile_scores(t):
                for half in range(2):
                    c0 = (t % 2) * 256 + half * P
                    last = mm(ps[:, 6 + t // 2, c0:c0 + P], qT[:, half, t * P:(t + 1) * P], keys[:, half],
                              start=True, stop=True)
                last.then_inc(scores_done, 1)

            def query(h, half):
                if half == 0:
                    pe.wait_ge(wpq_in, 16 * h + 16)
                if not isinstance(h, int) or h > 0:
                    pe.wait_ge(query_evac, 2 * h - 1 + half)
                for k in range(KD):
                    last = mm(ps[:, 4 + half], wpq[:, k, half * P:(half + 1) * P], h2T[:, k],
                              start=(k == 0), stop=(k == KD - 1))
                last.then_inc(query_done, 1)

            def key_scores(h):
                pe.wait_ge(query_evac, 2 * h + 2)
                if not isinstance(h, int) or h > 0:
                    pe.wait_ge(topk_done, 4 * h)
                for t in range(NT):
                    tile_scores(t)

            def expert_sums(h, t, s0=0, s1=TOPK):
                for s in range(s0, s1):
                    n = h * GROUP + t * TOPK + s
                    pe.wait_ge(diag_ready, n + 1)
                    if s == 0 and (not isinstance(h, int) or 4 * h + t >= 2):
                        pe.wait_ge(y_taken, 4 * h + t - 1)
                    for half in range(2):
                        last = mm(ps[:, 2 * (t % 2) + half], dg[:, s % 4],
                                  ring[(t * TOPK + s) % NB][:, D + half * 512:D + (half + 1) * 512],
                                  start=(s == 0), stop=(s == TOPK - 1))
                    last.then_inc(slot_summed, 1)

            def expert_head(h, more):
                if more:
                    query(h + 1, 0)
                expert_sums(h, 0)
                if more:
                    query(h + 1, 1)
                expert_sums(h, 1)
                if more:
                    key_scores(h + 1)
                expert_sums(h, 2)
                expert_sums(h, 3)

            project_out(0)
            project_out(1)
            transpose_h2(0)
            pe.wait_ge(wpq_in, 16)
            first_head(0, 1)
            project_out(2)
            transpose_h2(1)
            first_head(1, 2)
            project_out(3)
            pe.wait_ge(x1_ready, 5)
            expert_sums(0, 0, 0, TOPK // 2)
            transpose_h2(2)
            transpose_h2(3)
            first_head(2, 4)
            expert_sums(0, 0, TOPK // 2, TOPK)
            query(1, 0)
            query(1, 1)
            expert_sums(0, 1)
            key_scores(1)
            expert_sums(0, 2)
            expert_sums(0, 3)
            with pe.Fori(1, PH - 1) as h:
                expert_head(h, True)
            expert_head(PH - 1, False)

        @block.vector
        def _(dve):
            v = nc.vector
            tell, link = linker(dve, dve_step)
            def reduce_mods(n0, n1):
                for n in range(n0, n1):
                    dve.wait_ge(ada_in[n % 4], 16 * (n // 4 + 1))
                    for j in range(2):
                        m = 2 * n + j
                        tell(v.tensor_tensor_reduce(out=ada[:, n % 4, j], in0=ada[:, n % 4, j], in1=cact,
                                                    scale=1.0, scalar=0.0, op0=ALU.mult, op1=ALU.add,
                                                    accum_out=mod[:, m:m + 1]), ada_used)

            def normalise(t):
                dve.wait_ge(ms_ready, t + 1)
                link(v.reciprocal(rstd[:, t:t + 1], sd[:, t:t + 1]))
                tell(v.tensor_scalar(xn[:, t], X[:, t], rstd[:, t:t + 1], None, ALU.mult), xn_ready)

            def first_mods(k):
                reduce_mods(k, k + 1)
                dve.wait_ge(ada_used, 2 * k + 2)
                link(v.tensor_tensor(mod[:, 2 * k:2 * k + 2], mod[:, 2 * k:2 * k + 2], cols[:, 2 * k:2 * k + 2], ALU.add))
                link(v.scalar_tensor_tensor(out=mod[:, 2 * k:2 * k + 1], in0=mod[:, 2 * k:2 * k + 1], scalar=1.0,
                                            in1=cols[:, COL_GPM + k:COL_GPM + k + 1], op0=ALU.add, op1=ALU.mult),
                     mod1_ready)

            dve.wait_ge(c_act, 1)
            dve.wait_ge(small_in, 32)
            normalise(0)
            first_mods(0)
            normalise(1)
            normalise(2)
            first_mods(1)
            normalise(3)
            for k in range(2, KD):
                first_mods(k)
            dve.wait_ge(pos_in, 16)
            link(v.tensor_copy(ang, pos_i.bitcast(i32)))
            link(v.tensor_scalar(ang, ang, cols[:, COL_INV:COL_INV + 1], None, ALU.mult))
            red = turned[:, 0]
            for k, (buf, quarter) in enumerate(((turn, 0.25), (ang, 0.0))):
                link(v.tensor_scalar(red, ang, 1.0 / TWO_PI, quarter, ALU.mult, ALU.add))
                link(v.tensor_scalar(red, red, ROUND, ROUND, ALU.add, ALU.subtract))
                src = ang
                for part in (PI_A, PI_B, PI_C):
                    link(v.scalar_tensor_tensor(out=buf, in0=red, scalar=-part, in1=src, op0=ALU.mult, op1=ALU.add))
                    src = buf
                link(v.tensor_scalar(buf, buf, HALF_PI if k == 0 else 0.0, PI_MAX, ALU.add, ALU.min))
                link(v.tensor_scalar(buf, buf, -PI_MAX, None, ALU.max), angles)
            reduce_mods(8, 12)

            def rotate(out, straight, swapped, read):
                link(v.tensor_tensor(turned[:, 0], straight, cos_t, ALU.mult), read)
                link(v.tensor_tensor(turned[:, 1], swapped, sin_t, ALU.mult), read)
                link(v.tensor_tensor(out, turned[:, 0], turned[:, 1], ALU.add), rope_ready)

            dve.wait_ge(tables, 2)
            dve.wait_ge(kr_done, 2)
            rotate(krope, ps[:, 6], ps[:, 7], kr_read)
            reduce_mods(12, 16)
            for j, (k0, k1) in enumerate(((0, 3), (3, 5))):
                dve.wait_ge(ss_read, j + 1)
                link(v.reciprocal(tmp[:, j], tmp[:, j]))
                for k in range(k0, k1):
                    dve.wait_ge(proj_act, k + 1)
                    tell(v.tensor_tensor(latT[:, k], latT[:, k], tmp[:, j], ALU.mult), lat_ready)
            reduce_mods(16, 24)
            dve.wait_ge(ada_used, N_MOD)
            rest = slice(2 * KD, N_MOD)
            link(v.tensor_tensor(mod[:, rest], mod[:, rest], cols[:, rest], ALU.add))
            link(v.tensor_tensor(mod[:, GT1:GT1 + KD], mod[:, GT1:GT1 + KD], cols[:, COL_GQM:COL_GQM + KD], ALU.mult))
            link(v.scalar_tensor_tensor(out=mod[:, SC2:SC2 + KD], in0=mod[:, SC2:SC2 + KD], scalar=1.0,
                                        in1=cols[:, COL_GPF:COL_GPF + KD], op0=ALU.add, op1=ALU.mult))
            link(v.tensor_tensor(mod[:, GT2:GT2 + KD], mod[:, GT2:GT2 + KD], cols[:, COL_GQF:COL_GQF + KD], ALU.mult),
                 mods_ready)
            for i in range(4):
                dve.wait_ge(z_done, i + 1)
                tell(v.tensor_scalar(gate[:, i], ps[:, 4 + i], cols[:, COL_BG + i:COL_BG + i + 1], None, ALU.add),
                     z_read)
            for i in range(4):
                dve.wait_ge(gate_exp, i + 1)
                link(v.scalar_tensor_tensor(out=gate[:, i], in0=gate[:, i], scalar=0.0, in1=soft[:, i],
                                            op0=ALU.min, op1=ALU.subtract))
            for pair in range(2):
                dve.wait_ge(upq_done, 7 + pair)
                rotate(qr[:, pair], tmp[:, pair], ps[:, 2 + pair], up_dve)

            def running_sums(i):
                g_i = gate[:, i] if i < 2 else gate[:, i][:, ::-1]
                link(v.tensor_tensor_scan(g_i, scan_keep, g_i, 0.0, ALU.mult, ALU.add), sums_ready)
                if i >= 2:
                    dve.wait_ge(decay_ready, 2 * (i - 1))
                gc = gate[:, i].rearrange("p (c j) -> p c j", c=NCH)
                at_end = CHUNK - 1 if i < 2 else 0
                link(v.tensor_tensor(tmp[:, i % 2].rearrange("p (c j) -> p c j", c=NCH),
                                     gc[:, :, at_end:at_end + 1].to_broadcast([P, NCH, CHUNK]), gc, ALU.subtract),
                     sums_ready)

            def decayed_queries(i):
                dve.wait_ge(decay_dve, 2 * i + 2)
                for hh in range(2):
                    rows = slice(64 * hh, 64 * hh + 64)
                    tell(v.tensor_tensor(qdec[rows, i // 2, 2 * (i % 2) + hh], qgT[rows, i % 2], gtmp[rows, 0],
                                         ALU.mult), qdec_ready)

            dve.wait_ge(vg_done, NT)
            dve.wait_ge(proj_act, IN_TILES)
            scale = (NOPE + ROPE) ** -0.5
            for n in range(16 + 2):
                if n < 16:
                    dve.wait_ge(s_done, n + 1)
                    link(v.reduce_max(smax[:, n:n + 1], ps[:, n % 4], AX.X))
                    link(v.tensor_scalar(nmax[:, n:n + 1], smax[:, n:n + 1], -scale, None, ALU.mult), max_ready)
                m = n - 1
                if 0 <= m < 16:
                    dve.wait_ge(exp_done, m + 1)
                    link(v.reciprocal(rinv[:, m:m + 1], rsum[:, m:m + 1]))
                    tell(v.tensor_scalar(prob[:, m % 4], prob[:, m % 4], rinv[:, m:m + 1], None, ALU.mult),
                         prob_ready)
                if n % 4 == 1:
                    if n >= 5:
                        decayed_queries(n // 4 - 1)
                    if n < 16:
                        running_sums(n // 4)
            for i in range(4):
                dve.wait_ge(kd_done, i + 1)
                tell(v.tensor_copy(kdec[64:P, i, 1], ps[64:P, i]), kd_dve)
            for i in range(4):
                dve.wait_ge(ds_done, i + 1)
                b0 = 4 if i % 2 == 0 else 0
                for c in range(7):
                    add = ps[:, b0 + c // 2, (c % 2) * 256:(c % 2 + 1) * 256]
                    cur = state[:, i, c * 256:(c + 1) * 256]
                    if c == 0:
                        link(v.tensor_copy(cur, add))
                    else:
                        cc = c if i < 2 else 7 - c
                        link(v.scalar_tensor_tensor(out=cur, in0=state[:, i, (c - 1) * 256:c * 256],
                                                    scalar=edge[:, i, cc:cc + 1], in1=add,
                                                    op0=ALU.mult, op1=ALU.add),
                             state_ready if c == 6 else dve_step)
            for n in range(8):
                d, h = n // GLA_H, n % GLA_H
                dve.wait_ge(att_done, (n | 1) + 1)
                for par in range(2):
                    rows = slice(64 * par, 64 * par + 64)
                    tell(v.tensor_tensor(
                        att[d][rows, h].rearrange("p (t c) -> p t c", t=NT)[:, :, 64 * par:64 * par + 64],
                        ps[rows, 4 + n // 2, (n % 2) * 256:(n % 2 + 1) * 256].rearrange("p (t c) -> p t c", t=NT),
                        tri[rows, d:d + 1, :].to_broadcast([64, NT, CHUNK]), ALU.mult), att_ready)
            dve.wait_ge(og_done, GLA_H)
            for u in range(8):
                m = (GT1, SC2, SH2, GT2)[u // 2] + 4 * (u % 2)
                tell(v.tensor_tensor(diag8[:, u].rearrange("p (k j) -> p k j", k=4),
                                     ident.unsqueeze(1).to_broadcast([P, 4, P]),
                                     mod[:, m:m + 4].unsqueeze(2).to_broadcast([P, 4, P]), ALU.mult), diag_cols)
            for h in range(GLA_H):
                dve.wait_ge(gsd_ready, h + 1)
                link(v.reciprocal(grs[:, h % 2], grs[:, h % 2]))
                link(v.tensor_tensor(grs[:, h % 2], ps[:, h], grs[:, h % 2], ALU.mult))
                link(v.scalar_tensor_tensor(out=mixT[:, 4 + h], in0=grs[:, h % 2], scalar=cols[:, COL_GGLA:COL_GGLA + 1],
                                            in1=rT[:, h], op0=ALU.mult, op1=ALU.mult), mix_ready)
            dve.wait_ge(bc_evac, 8)

            def norm_y(t):
                b0 = 2 * (t % 2)
                dve.wait_ge(ssy_ready, t + 1)
                link(v.reciprocal(rstd[:, t:t + 1], sd[:, t:t + 1]))
                link(v.scalar_tensor_tensor(out=h2[:, t].rearrange("p (a b) -> p a b", a=2),
                                            in0=ps[:, b0:b0 + 2], scalar=rstd[:, t:t + 1],
                                            in1=bcast[:, 0].rearrange("p (a b) -> p a b", a=2),
                                            op0=ALU.mult, op1=ALU.mult), x1_ready)
                link(v.tensor_tensor(X[:, t], X[:, t], h2[:, t], ALU.add), x1_ready)

            def norm_x(t):
                dve.wait_ge(ssx_ready, t + 1)
                link(v.reciprocal(rstdb[:, t:t + 1], sdb[:, t:t + 1]))
                link(v.scalar_tensor_tensor(out=h2[:, t], in0=X[:, t], scalar=rstdb[:, t:t + 1], in1=bcast[:, 1],
                                            op0=ALU.mult, op1=ALU.mult))
                link(v.tensor_tensor(h2[:, t], h2[:, t], bcast[:, 2], ALU.add), h2_ready)

            STAGES = 13

            def topk_stage(h, t, k):
                step = [2 * k]

                def link(ins, alone=False):
                    step[0] += 1
                    ins.then_inc(topk_step, 1)
                    value = (4 * h + t) * (2 * STAGES - 1) + step[0]
                    if alone:
                        hold(dve, topk_step, value)
                    else:
                        dve.wait_ge(topk_step, value)

                s = [ps[:, 6 + t // 2, (t % 2) * 256 + j * P:(t % 2) * 256 + (j + 1) * P] for j in range(2)]
                lo, hi = slice(0, 8), slice(8, 16)
                cand3 = cand.rearrange("p (a b) -> p a b", a=TOPK)
                oh = onehot.rearrange("p a k j -> p (a k) j")
                if k == 0:
                    alone = isinstance(h, int) and h == 0 and t < 2
                    hold(dve, scores_done, 4 * h + (t if alone else t | 1) + 1)
                    link(v.max(v12[:, 0, lo], s[0]), True)
                    link(v.max(v12[:, 1, lo], s[1]), True)
                elif k == 1:
                    link(v.max_index(i12[:, 0, lo], v12[:, 0, lo], s[0]), True)
                    link(v.max_index(i12[:, 1, lo], v12[:, 1, lo], s[1]), True)
                elif k == 2:
                    link(v.match_replace(srest[:, 0], v12[:, 0, lo], s[0], NEG), True)
                    link(v.match_replace(srest[:, 1], v12[:, 1, lo], s[1], NEG), True)
                elif k == 3:
                    link(v.max(v12[:, 0, hi], srest[:, 0]), True)
                    link(v.max(v12[:, 1, hi], srest[:, 1]), True)
                elif k == 4:
                    link(v.max_index(i12[:, 0, hi], v12[:, 0, hi], srest[:, 0]), True)
                    link(v.max_index(i12[:, 1, hi], v12[:, 1, hi], srest[:, 1]))
                elif k == 5:
                    link(v.tensor_tensor(cand3, v12[:, 0].unsqueeze(2).to_broadcast([P, TOPK, TOPK]),
                                         v12[:, 1:2].to_broadcast([P, TOPK, TOPK]), ALU.add), True)
                    link(v.max(tops[:, t, lo], cand), True)
                elif k == 6:
                    link(v.max_index(posn[:, lo], tops[:, t, lo], cand), True)
                    link(v.match_replace(crest, tops[:, t, lo], cand, NEG), True)
                elif k == 7:
                    link(v.max(tops[:, t, hi], crest), True)
                    link(v.max_index(posn[:, hi], tops[:, t, hi], crest))
                elif k == 8:
                    link(v.tensor_single_scalar(pab[:, 0], posn, 4, ALU.logical_shift_right))
                    link(v.tensor_single_scalar(pab[:, 1], posn, 15, ALU.bitwise_and))
                elif k == 9:
                    link(v.tensor_copy(pabf, pab))
                    link(v.tensor_copy(i12f, i12))
                elif k == 10:
                    link(v.tensor_tensor(oh, pabf.rearrange("p a k -> p (a k)").unsqueeze(2).to_broadcast([P, 32, TOPK]),
                                         iota.unsqueeze(1).to_broadcast([P, 32, TOPK]), ALU.is_equal))
                    link(v.tensor_tensor(onehot[:, 0], onehot[:, 0], i12f[:, 0:1].to_broadcast([P, TOPK, TOPK]),
                                         ALU.mult))
                elif k == 11:
                    link(v.tensor_tensor(onehot[:, 1], onehot[:, 1], i12f[:, 1:2].to_broadcast([P, TOPK, TOPK]),
                                         ALU.mult))
                    link(v.tensor_reduce(sel.rearrange("p a k -> p (a k)"), oh, AX.X, ALU.add))
                else:
                    link(v.scalar_tensor_tensor(out=eidx[:, t], in0=sel[:, 0], scalar=float(NKEYS), in1=sel[:, 1],
                                                op0=ALU.mult, op1=ALU.add))
                    v.tensor_scalar(nmx[:, t:t + 1], tops[:, t, 0:1], -1.0, None, ALU.mult).then_inc(topk_done, 1)

            def finish_gates(h, t):
                dve.wait_ge(topk_exp, 4 * h + t + 1)
                v.reciprocal(tinv[:, t:t + 1], tsum[:, t:t + 1]).then_inc(tinv_done, 1)
                dve.wait_ge(tinv_done, 4 * h + t + 1)
                v.tensor_scalar(gates[:, t], etop[:, t], tinv[:, t:t + 1], None, ALU.mult).then_inc(gates_ready, 1)

            def take_sums(h, t):
                dve.wait_ge(slot_summed, h * GROUP + (t + 1) * TOPK)
                if not isinstance(h, int) or h > 0:
                    dve.wait_ge(y_taken, 4 * h + t - 3)
                y = yacc[:, t].rearrange("p (a b) -> p a b", a=2)
                sums = ps[:, 2 * (t % 2):2 * (t % 2) + 2]
                if isinstance(h, int) and h == 0 and t < NT - 1:
                    v.tensor_copy(y, sums).then_inc(y_taken, 1)
                else:
                    v.tensor_tensor(y, y, sums, ALU.add).then_inc(y_taken, 1)

            def dot(h, t, s):
                b = (t * TOPK + s) % NB
                dve.wait_ge(rows_in[b], 16 * (h * (GROUP // NB) + (t * TOPK + s) // NB + 1))
                v.tensor_tensor_reduce(out=ring[b][:, 0:D], in0=ring[b][:, 0:D], in1=h2[:, t], scale=1.0,
                                       scalar=0.0, op0=ALU.mult, op1=ALU.add,
                                       accum_out=adot[:, t, s:s + 1]).then_inc(dots_done, 1)

            def score_experts(h, more, tiles=range(NT)):
                for t in tiles:
                    ahead = (h, t + 2) if t < 2 else (h + 1, t - 2)
                    following = (h, t + 1) if t < 3 else (h + 1, 0)
                    for s in range(TOPK):
                        dot(h, t, s)
                        if s >= TOPK - STAGES and (more or t < 2):
                            topk_stage(*ahead, s - (TOPK - STAGES))
                        if s == 4 and t > 0:
                            take_sums(h, t - 1)
                        if s == 4 and t == 0:
                            take_sums(h - 1, NT - 1)
                        if s == 11 and (more or t < 3):
                            finish_gates(*following)
                        if s == 14 and not more and t > 0:
                            finish(t - 1)

            def finish(t):
                dve.wait_ge(ssf_ready, t + 1)
                link(v.reciprocal(rstd[:, t:t + 1], sd[:, t:t + 1]))
                link(v.scalar_tensor_tensor(out=fout[:, t], in0=yacc[:, t], scalar=rstd[:, t:t + 1], in1=bcast[:, 3],
                                            op0=ALU.mult, op1=ALU.mult))
                link(v.tensor_tensor(fout[:, t], fout[:, t], X[:, t], ALU.add), out_ready)

            for t in range(2):
                norm_y(t)
                norm_x(t)
            for k in range(STAGES):
                topk_stage(0, 0, k)
            norm_y(2)
            norm_x(2)
            finish_gates(0, 0)
            for s in range(3):
                dot(0, 0, s)
            for k in range(STAGES):
                topk_stage(0, 1, k)
            for s in range(3, 6):
                dot(0, 0, s)
            norm_y(3)
            for s in range(6, 8):
                dot(0, 0, s)
            norm_x(3)
            for s in range(8, TOPK):
                dot(0, 0, s)
            for k in range(STAGES):
                topk_stage(0, 2, k)
            finish_gates(0, 1)
            dve.wait_ge(y_zero, 1)
            score_experts(0, True, range(1, NT))
            with dve.Fori(1, PH - 1) as h:
                score_experts(h, True)
            score_experts(PH - 1, False)
            take_sums(PH - 1, NT - 1)
            finish(3)


def kernel(x, c, positions, w_ada, b_ada, g_pre_mix, g_post_mix, w_in, g_q_latent, w_q_up,
           g_kv_latent, w_kv_up, w_gate_fwd, b_gate_fwd, w_gate_bwd, b_gate_bwd, g_gla_norm,
           w_out, g_pre_ffn, g_post_ffn, w_peer_q, sub_keys_1, sub_keys_2, expert_u, expert_v):
    import numpy as np
    import concourse.bacc as bacc
    from concourse import mybir as mb
    from concourse.bass_utils import run_bass_kernel_spmd

    f = np.float32

    def feature_cols(vec):
        return np.asarray(vec).reshape(-1, P).T

    def k_major(w, n):
        return np.asarray(w).reshape(-1, P, w.shape[-1]).transpose(1, 0, 2)

    p = np.arange(P)
    inv = np.float64(THETA) ** (-(p % 32) / 32.0)
    sign = np.where(p % 64 < 32, -1.0, 1.0)
    own = np.stack([inv, sign, np.full(P, EPS)], 1).astype(f)
    j, i = (p % 64)[:, None], np.arange(CHUNK)[None]
    const = np.concatenate([np.eye(P), np.ones((P, P)), j <= i, j >= i,
                            np.broadcast_to(np.arange(SEQ) % CHUNK != 0, (P, SEQ)),
                            np.broadcast_to(np.arange(TOPK), (P, TOPK))], 1).astype(f)

    b6 = np.asarray(b_ada)[0].reshape(6, D)
    mods = [feature_cols(b6[m]) for m in MOD_ORDER]
    cols = np.concatenate([np.stack(mods[:2], 2).reshape(P, 2 * KD)] + mods[2:]
                          + [feature_cols(g[0]) for g in (g_pre_mix, g_post_mix, g_pre_ffn, g_post_ffn)]
                          + [feature_cols(g_q_latent[0]), feature_cols(g_kv_latent[0]),
                             feature_cols(b_gate_fwd[0]), feature_cols(b_gate_bwd[0]),
                             feature_cols(g_gla_norm[0]), own], 1)
    ada = np.asarray(w_ada)[0].reshape(D, 6, KD, P)[:, list(MOD_ORDER)]
    ada = np.concatenate([ada[:, :2].transpose(0, 2, 1, 3).reshape(D, 2 * KD, P),
                          ada[:, 2:].reshape(D, 4 * KD, P)], 1)
    ada = ada.reshape(D, 24, 2, P).transpose(3, 1, 2, 0)

    w = np.asarray(w_in)[0]
    sizes = (Q_RANK, KV_RANK, ROPE, GLA_H * DK, GLA_H * DK, GLA_H * DV, GATE_RANK, GATE_RANK, GLA_H * DV)
    at = np.concatenate([[0], np.cumsum(sizes)])
    cq, ckv, kr, qg, kg, vg, gf, gb, r = (w[:, at[n]:at[n + 1]] for n in range(9))
    pad = np.zeros((D, P - ROPE - 2 * GATE_RANK), f)
    tiles = np.concatenate([cq, ckv, kr, gf, gb, pad, qg, kg, r], 1)
    first, vals = (m.reshape(4, 2, P, 512).transpose(2, 0, 1, 3).reshape(P, 4, 1024)
                   for m in (tiles[:, :4 * P], vg))
    tiles = tiles.reshape(KD, P, IN_TILES, P).transpose(1, 2, 0, 3).reshape(P, IN_TILES, KD * P)
    tiles = np.concatenate([first, tiles[:, 4:]], 1)
    a, b = np.arange(P)[:, None], np.arange(P)[None]
    other = b - b % 64 + (b + 32) % 64
    perm = np.concatenate([a == other, a == b % 64, a == (b + 32) % 64], 1).astype(f)
    win = np.concatenate([tiles, vals], 1)

    wq = np.asarray(w_q_up)[0].reshape(Q_RANK, MLA_H, NOPE + ROPE)
    nope, rp = wq[:, :, :NOPE], wq[:, :, NOPE:]
    units = [nope[:, h] for h in range(4)] + [rp[:, 2 * k:2 * k + 2].reshape(Q_RANK, P) for k in range(2)]
    wqup = np.stack(units, 1).reshape(3, P, 6, P).transpose(1, 0, 2, 3)
    wkv = np.asarray(w_kv_up)[0].reshape(KV_RANK, MLA_H, NOPE + DV)
    wkv = np.concatenate([wkv[:, :, :NOPE].reshape(KV_RANK, 512), wkv[:, :, NOPE:].reshape(KV_RANK, 512)], 1)
    wkvup = k_major(wkv, 1024)
    wgate = np.zeros((2 * GATE_RANK, 2, 2, P), f)
    wgate[:GATE_RANK, 0] = np.asarray(w_gate_fwd)[0].reshape(GATE_RANK, 2, P)
    wgate[GATE_RANK:, 1] = np.asarray(w_gate_bwd)[0].reshape(GATE_RANK, 2, P)
    wpq = np.asarray(w_peer_q)[0].reshape(KD, P, PH, DKEY).transpose(2, 1, 0, 3)
    keys = np.stack([np.asarray(sub_keys_1)[0].T, np.asarray(sub_keys_2)[0].T], 1)
    uv = np.concatenate([np.asarray(expert_u)[0], np.asarray(expert_v)[0]], 1)

    ins = dict(x=np.asarray(x)[0], c=np.asarray(c)[0], pos=np.asarray(positions)[0], ada=ada, cols=cols,
               const=const, keys=keys, win=win, perm=perm, wqup=wqup, wkvup=wkvup, wgate=wgate,
               wout=k_major(np.asarray(w_out)[0], D), wpq=wpq, uv=uv)
    ins = {k: np.ascontiguousarray(a) for k, a in ins.items()}
    nc = bacc.Bacc("TRN2", target_bir_lowering=False, num_devices=1)
    aps = [nc.dram_tensor(f"in_{k}", a.shape, mb.dt.from_np(a.dtype), kind="ExternalInput").ap()
           for k, a in ins.items()]
    out = nc.dram_tensor("out_y", (SEQ, D), mb.dt.float32, kind="ExternalOutput").ap()
    build(nc, *aps, out)
    r = run_bass_kernel_spmd(nc, [{f"in_{k}": a for k, a in ins.items()}], core_ids=[0])
    return r.results[0]["out_y"].reshape(1, SEQ, D)
```

```python
import concourse.bass as bass
from concourse import mybir
from contextlib import ExitStack

P = 128
D, SEQ = 1024, 512
KD, NT = D // P, SEQ // P
Q_RANK, KV_RANK = 384, 256
MLA_H, NOPE, ROPE, DV = 4, 128, 64, 128
GLA_H, DK, CHUNK = 4, 64, 64
NCH = SEQ // CHUNK
GATE_RANK, GATE_NORM = 16, 16.0
PH, NKEYS, DKEY, TOPK = 8, 128, 256, 16
EPS = 1e-6
THETA = 10000.0
TWO_PI = 6.283185307179586
PI_A = 6.28125
PI_B = 0.001934051513671875
PI_C = TWO_PI - PI_A - PI_B
HALF_PI = 1.5707963267948966
PI_MAX = 3.1415925
ROUND = 12582912.0
NEG = -3.0e38

N_MOD = 6 * KD
COL_GPM, COL_GQM, COL_GPF, COL_GQF = N_MOD, N_MOD + 8, N_MOD + 16, N_MOD + 24
COL_GQL = N_MOD + 32
COL_GKVL = COL_GQL + 3
COL_BG = COL_GKVL + 2
COL_GGLA = COL_BG + 4
COL_INV, COL_SIGN, COL_EPS = COL_GGLA + 1, COL_GGLA + 2, COL_GGLA + 3
NCOLS = COL_EPS + 1
GT1, SC2, SH2, GT2 = (k * KD for k in range(2, 6))
MOD_ORDER = (1, 0, 2, 4, 3, 5)

K_ID, K_ONES, K_TRI, K_SCAN, K_IOTA = 0, P, 2 * P, 3 * P, 3 * P + SEQ
NCONST = K_IOTA + TOPK

IN_TILES = 10
IN_CHUNKS = IN_TILES + 8
KRG, QG, KG = 5, 6, 8

NB = 8
GROUP = NT * TOPK

O_COLS = 0
O_CONST = O_COLS + NCOLS + (NCOLS & 1)
O_KEYS = O_CONST + NCONST
O_X = 1280
O_SMALL = O_X + NT * D
O_UP = 5600
O_W = O_UP + 5120
O_ADA = O_W + 8 * 1024
O_H1T = O_ADA + 8192
O_LAT = O_H1T + KD * SEQ
O_KROPE = O_LAT + 5 * SEQ
O_QG = O_KROPE + SEQ
O_KG = O_QG + 2 * SEQ
O_R = O_KG + 2 * SEQ
O_VG = O_R + 4 * SEQ
O_GL = O_VG + 4 * SEQ
O_E = O_GL + SEQ
O_TAB = O_E + 7 * 1024
O_TMP = O_TAB + 2 * SEQ
O_END = O_TMP + 2 * SEQ
O_PERM = O_END + 3 * SEQ
SBUF_WORDS = 53200
O_YACC = O_UP
O_DIAG = O_YACC + NT * D
O_FOUT = O_W
O_BC = O_ADA
O_SLOTS = [((O_H1T, O_ADA + 4 * D, O_LAT, O_LAT + 4 * D)[b // 2]) + (b % 2) * 2 * D for b in range(NB)]
O_JUNK = O_LAT + 4 * 2 * D
O_H2 = O_GL
O_H2T = O_H2 + NT * D
O_TOPK = O_H2T + KD * SEQ
O_QT = 50128
O_WQ = SBUF_WORDS - 2048


def build(nc, x_d, c_d, pos_d, ada_d, cols_d, const_d, keys_d, win_d, perm_d, wqup_d, wkvup_d, wgate_d,
          wout_d, wpq_d, uv_d, out_d):
    f32, u32, i32 = mybir.dt.float32, mybir.dt.uint32, mybir.dt.int32
    f32r = mybir.dt.float32r
    ACT, ALU, AX = mybir.ActivationFunctionType, mybir.AluOpType, mybir.AxisListType
    ctx = ExitStack()
    with ctx:
        A = ctx.enter_context(nc.sbuf_tensor("arena", [P, SBUF_WORDS], f32))
        ps = ctx.enter_context(nc.psum_tensor("ps", [P, 8, 512], f32))

        def sem(name):
            return ctx.enter_context(nc.semaphore(name))

        def at(off, *shape):
            n = 1
            for s in shape:
                n *= s
            v = A[:, off:off + n]
            if len(shape) == 2:
                return v.rearrange("p (a b) -> p a b", a=shape[0])
            if len(shape) == 3:
                return v.rearrange("p (a b c) -> p a b c", a=shape[0], b=shape[1])
            return v

        cols = at(O_COLS, NCOLS)
        const = at(O_CONST, NCONST)
        ident, ones = const[:, K_ID:K_ID + P], const[:, K_ONES:K_ONES + P]
        tri = const[:, K_TRI:K_TRI + 2 * CHUNK].rearrange("p (d i) -> p d i", d=2)
        scan_keep = const[:, K_SCAN:K_SCAN + SEQ]
        iota = const[:, K_IOTA:K_IOTA + TOPK]
        keys = at(O_KEYS, 2, NKEYS)
        X = at(O_X, NT, D)
        small = at(O_SMALL, 224)
        mod = small[:, 0:N_MOD]
        ss, sd, rstd = small[:, 48:52], small[:, 52:56], small[:, 56:60]
        nmax, rsum, rinv = small[:, 64:80], small[:, 80:96], small[:, 96:112]
        edge = small[:, 112:144].rearrange("p (i c) -> p i c", i=4)
        ssb, sdb, rstdb = small[:, 144:148], small[:, 148:152], small[:, 152:156]
        smax = small[:, 160:176]
        gss, gsd, grstd = (small[:, o:o + NT * GLA_H].rearrange("p (t h) -> p t h", t=NT) for o in (176, 192, 208))
        eps = cols[:, COL_EPS:COL_EPS + 1]

        cact = at(O_E, D)
        craw = at(O_TAB, D)
        xn = at(O_E + D, NT, D)
        ada = at(O_ADA, 4, 2, D)
        wring = at(O_W, 8, 1024)
        wqup, wkvup = at(O_UP, 3, 6, P), at(O_UP + 3072, 2, 1024)
        h1T = at(O_H1T, KD, SEQ)
        latT = at(O_LAT, 5, SEQ)
        krope = at(O_KROPE, SEQ)
        qgT, kgT = at(O_QG, 2, SEQ), at(O_KG, 2, SEQ)
        rg, vg = at(O_R, NT, SEQ), at(O_VG, NT, SEQ)
        krgT = at(O_GL, SEQ)
        perm = at(O_PERM, 3 * P)
        swap_q, dup_k, swap_k = (perm[:, k * P:(k + 1) * P] for k in range(3))
        qn, qr, kn, vm = (at(O_E, 4, SEQ), at(O_E + 2048, 2, SEQ), at(O_E + 3072, 4, SEQ),
                          at(O_E + 5120, NT, SEQ))
        cos_t, sin_t = at(O_TAB, SEQ), at(O_TAB + SEQ, SEQ)
        tmp = at(O_TMP, 2, SEQ)
        latsq = [at(O_R + k * SEQ, SEQ) for k in range(4)] + [at(O_END + SEQ, SEQ)]
        arena_at = nc.sbuf_base - 4 * SBUF_WORDS

        def rounded(name, off, n):
            return nc.alloc_sbuf_tensor_at(name, [P, n], f32r, offset=arena_at + 4 * off)[:, :]

        h1hi = [rounded(f"h1hi{k}", O_E + D + k * SEQ, SEQ) for k in range(KD)]
        h1lo = [rounded(f"h1lo{k}", O_H1T + k * SEQ, SEQ) for k in range(KD)]
        whi = [rounded(f"whi{k}", (O_E + 5 * D, O_VG)[k // 2] + (k % 2) * 1024, 1024) for k in range(4)]
        wlo = [rounded(f"wlo{k}", O_W + k * 1024, 1024) for k in range(8)]
        wgate = at(O_END, 2, 2, P)
        turned = at(O_PERM + 3 * P, 2, SEQ)
        pos_i, ang, turn = at(O_QG, SEQ), at(O_KG, SEQ), at(O_KG + SEQ, SEQ)
        prob, probT = at(O_ADA, 4, SEQ), at(O_ADA + 2048, NT, SEQ)
        mixT = at(O_UP, 8, SEQ)
        gate = at(O_W + 2048, 4, SEQ)
        soft = at(O_W + 4096, 4, SEQ)
        qdec = at(O_H1T, 2, GLA_H, SEQ)
        kinv = at(O_ADA + 4096, 4, SEQ)
        kdecT = at(O_ADA + 6144, 4, SEQ)
        gtmp = at(O_END, 3, SEQ)
        kdec = at(O_W, 4, 2, 512)
        state = at(O_E, 4, 7 * DV)
        att = [at(O_QG, GLA_H, 512), at(O_LAT, GLA_H, 512)]
        gsq = at(O_TMP, 2, SEQ)
        gmix = at(O_END, 2, SEQ)
        col_diag = at(O_UP + 4 * SEQ, 4, 512)
        bcast = at(O_BC, 4, D)
        wout = at(O_W, KD, D)
        h2, h2T = at(O_H2, NT, D), at(O_H2T, KD, SEQ)
        junk = at(O_JUNK, 1, D)
        yacc, ring = at(O_YACC, NT, D), [at(o, 2 * D) for o in O_SLOTS]
        wpq, qT = at(O_WQ, KD, DKEY), at(O_QT, 2, SEQ)
        fout = at(O_FOUT, NT, D)
        o = [O_TOPK]

        def small_buf(n):
            o[0] += n
            assert o[0] <= O_QT
            return A[:, o[0] - n:o[0]]

        v12 = small_buf(32).rearrange("p (a b) -> p a b", a=2)
        i12 = small_buf(32).bitcast(u32).rearrange("p (a b) -> p a b", a=2)
        i12f = small_buf(32).rearrange("p (a b) -> p a b", a=2)
        srest = small_buf(256).rearrange("p (a b) -> p a b", a=2)
        cand, crest = small_buf(256), small_buf(256)
        tops = small_buf(NT * TOPK).rearrange("p (a b) -> p a b", a=NT)
        posn = small_buf(16).bitcast(u32)
        pab = small_buf(32).bitcast(u32).rearrange("p (a b) -> p a b", a=2)
        pabf = small_buf(32).rearrange("p (a b) -> p a b", a=2)
        sel = small_buf(32).rearrange("p (a b) -> p a b", a=2)
        eidx = small_buf(NT * TOPK).bitcast(u32).rearrange("p (a b) -> p a b", a=NT)
        etop = small_buf(NT * TOPK).rearrange("p (a b) -> p a b", a=NT)
        gates = small_buf(NT * TOPK).rearrange("p (a b) -> p a b", a=NT)
        adot = small_buf(NT * TOPK).rearrange("p (a b) -> p a b", a=NT)
        agelu = small_buf(NT * TOPK).rearrange("p (a b) -> p a b", a=NT)
        wexp = small_buf(NT * TOPK).rearrange("p (a b) -> p a b", a=NT)
        nmx, tsum, tinv = small_buf(NT), small_buf(NT), small_buf(NT)
        dg, onehot = at(O_DIAG, 4, P), at(O_DIAG + 4 * P, 2, TOPK, TOPK)

        perm_in, c_in, cols_in, const_in, up_in = (sem("perm_in"), sem("c_in"), sem("cols_in"),
                                                    sem("const_in"), sem("up_in"))
        x_in = [sem(f"x_in{t}") for t in range(NT)]
        ada_in, ada_used = [sem(f"ada_in{k}") for k in range(4)], sem("ada_used")
        ada_late = [sem(f"ada_late{k}") for k in range(4)]
        win_in = [sem(f"win_in{k}") for k in range(8)]
        wout_in, wpq_in = sem("wout_in"), sem("wpq_in")
        dve_step, act_step, pool_step = sem("dve_step"), sem("act_step"), sem("pool_step")
        c_act, ms_ready, xn_ready = sem("c_act"), sem("ms_ready"), sem("xn_ready")
        xT_done, mod1_ready, mods_ready = sem("xT_done"), sem("mod1_ready"), sem("mods_ready")
        h1_ready, pos_in = sem("h1_ready"), sem("pos_in")
        kr_done, kr_read = sem("kr_done"), sem("kr_read")
        rows_used, h1_hi, h1_lo = sem("rows_used"), sem("h1_hi"), sem("h1_lo")
        w_hi, w_lo, gate_chunk = sem("w_hi"), sem("w_lo"), sem("gate_chunk")
        angles, tables = sem("angles"), sem("tables")
        proj_act = sem("proj_act")
        lat_done, sq_ready, sq_summed, ss_done, ss_read = (
            sem("lat_done"), sem("sq_ready"), sem("sq_summed"), sem("ss_done"), sem("ss_read"))
        lat_ready, z_done, z_read, gate_exp = (sem("lat_ready"), sem("z_done"), sem("z_read"),
                                               sem("gate_exp"))
        vg_done, vg_evac = sem("vg_done"), sem("vg_evac")
        rg_done, rg_evac = sem("rg_done"), sem("rg_evac")
        upq_done, up_act, up_dve = sem("upq_done"), sem("up_act"), sem("up_dve")
        s_done, max_ready, exp_done, prob_ready = (sem("s_done"), sem("max_ready"), sem("exp_done"),
                                                   sem("prob_ready"))
        pt_done, pt_evac, o_done, o_evac = sem("pt_done"), sem("pt_evac"), sem("o_done"), sem("o_evac")
        zeros_ready, sums_ready, decay_ready = (sem("zeros_ready"), sem("sums_ready"),
                                                sem("decay_ready"))
        qdec_ready, kdec_ready = sem("qdec_ready"), sem("kdec_ready")
        decay_dve = sem("decay_dve")
        kd_done, kd_act, kd_dve = sem("kd_done"), sem("kd_act"), sem("kd_dve")
        ds_done, state_ready = sem("ds_done"), sem("state_ready")
        zeros2, att_done, att_ready = sem("zeros2"), sem("att_done"), sem("att_ready")
        og_done, gsq_ready, gss_ready, gsd_ready, mix_ready, mixT_done, mixT_evac = (
            sem("og_done"), sem("gsq_ready"), sem("gss_ready"), sem("gsd_ready"), sem("mix_ready"),
            sem("mixT_done"), sem("mixT_evac"))
        diag_cols, bc_done, bc_evac = sem("diag_cols"), sem("bc_done"), sem("bc_evac")
        y_done, ssy_ready, x1_ready, ssx_ready = (sem("y_done"), sem("ssy_ready"), sem("x1_ready"),
                                                  sem("ssx_ready"))
        h2_ready, h2T_done, h2T_evac = sem("h2_ready"), sem("h2T_done"), sem("h2T_evac")
        query_done, query_evac, scores_done = sem("query_done"), sem("query_evac"), sem("scores_done")
        topk_step, topk_done, topk_exp, gates_ready = (sem("topk_step"), sem("topk_done"),
                                                       sem("topk_exp"), sem("gates_ready"))
        rows_in = [sem(f"rows_in{b}") for b in range(NB)]
        dots_done, gelu_done, weight_done, diag_ready = (sem("dots_done"), sem("gelu_done"),
                                                         sem("weight_done"), sem("diag_ready"))
        slot_summed, y_taken, y_zero = sem("slot_summed"), sem("y_taken"), sem("y_zero")
        first_query, first_evac = sem("first_query"), sem("first_evac")
        rope_ready, tinv_done = sem("rope_ready"), sem("tinv_done")
        ssf_ready, out_ready, out_written = sem("ssf_ready"), sem("out_ready"), sem("out_written")

        def linker(eng, own):
            count = {}

            def tell(ins, s=own):
                count[s.name] = count.get(s.name, 0) + 1
                ins.then_inc(s, 1)

            def link(ins, s=own):
                tell(ins, s)
                eng.wait_ge(s, count[s.name])

            return tell, link

        def hold(eng, s, value):
            eng.wait_ge(s, value)
            if not isinstance(value, int):
                eng.nop(nofuse=True)

        def wait_unit_evacuated(pe, u):
            if u in (6, 7):
                pe.wait_ge(up_dve, 2 * (u - 5))
            else:
                pe.wait_ge(up_act, u + 1 if u < 6 else u - 1)

        block = ctx.enter_context(nc.Block())

        @block.sync
        def _(sp):
            def load_x(t):
                sp.dma_start(X[:, t], x_d[t * P:(t + 1) * P, :]).then_inc(x_in[t], 16)

            def load_win(n):
                if n >= 8:
                    sp.wait_ge(lat_done, 1 if n < 11 else n - 7)
                sp.dma_start(wring[:, n % 8], win_d[:, n, :]).then_inc(win_in[n % 8], 16)

            sp.dma_start(cols, cols_d).then_inc(cols_in, 16)
            sp.dma_start(craw, c_d.partition_broadcast(P)).then_inc(c_in, 16)
            load_x(0)
            load_x(1)
            sp.dma_start(const, const_d).then_inc(const_in, 16)
            load_x(2)
            load_x(3)
            load_win(0)
            for n in range(1, 8):
                sp.wait_ge(ada_used, min(4 * n - 2, 16))
                load_win(n)
            sp.dma_start(pos_i.bitcast(i32), pos_d.partition_broadcast(P)).then_inc(pos_in, 16)

            def load_ada(n):
                sp.wait_ge(ada_used, 2 * (n - 3))
                sp.dma_start(ada[:, n % 4], ada_d[:, n, :, :]).then_inc(ada_late[n % 4], 16)

            for n in range(8, 12):
                load_ada(n)
            sp.dma_start(perm, perm_d).then_inc(perm_in, 16)
            sp.dma_start(wgate[64:96], wgate_d).then_inc(perm_in, 16)
            for n in range(8, 12):
                load_win(n)
            sp.dma_start(keys, keys_d).then_inc(up_in, 16)
            sp.dma_start(wqup, wqup_d).then_inc(up_in, 16)
            sp.dma_start(wkvup, wkvup_d).then_inc(up_in, 16)
            for n in range(12, IN_CHUNKS):
                load_win(n)
                load_ada(n)
            for n in range(IN_CHUNKS, 24):
                load_ada(n)
            sp.wait_ge(ds_done, 4)
            sp.dma_start(wout, wout_d).then_inc(wout_in, 16)
            sp.wait_ge(mixT_done, NT)
            sp.dma_start(wpq, wpq_d[0]).then_inc(wpq_in, 16)
            with sp.Fori(1, PH) as h:
                sp.wait_ge(query_done, h * 2)
                sp.dma_start(wpq, wpq_d[bass.ds(h, 1)].rearrange("o p k n -> p (o k) n")).then_inc(wpq_in, 16)
            for t in range(NT):
                sp.wait_ge(out_ready, t + 1)
                sp.dma_start(out_d[t * P:(t + 1) * P, :], fout[:, t]).then_inc(out_written, 16)
            sp.wait_ge(out_written, 16 * NT)

        @block.gpsimd
        def _(pool):
            g = nc.gpsimd
            _, link = linker(pool, pool_step)
            pool.wait_ge(c_in, 16)
            for n in range(8):
                if n == 1:
                    pool.wait_ge(x_in[1], 16)
                if n >= 4:
                    pool.wait_ge(ada_used, 2 * (n - 3))
                g.dma_start(ada[:, n % 4], ada_d[:, n, :, :]).then_inc(ada_in[n % 4], 16)
            for n in range(4, IN_CHUNKS):
                pool.wait_ge(w_hi, n - 3)
                link(g.tensor_tensor(wlo[n % 8], wring[:, n % 8], whi[n % 4].bitcast(f32), ALU.subtract), w_lo)
            pool.wait_ge(vg_done, NT)
            for d in range(2):
                for h in range(GLA_H):
                    r0 = 64 * (1 - h % 2)
                    link(g.memset(qdec[r0:r0 + 64, d, h], 0.0), zeros_ready)
            for i in range(4):
                pool.wait_ge(decay_ready, 2 * i + 1)
                link(g.tensor_tensor(kinv[:, i], kgT[:, i % 2], gtmp[:, 1], ALU.mult), kdec_ready)
                pool.wait_ge(decay_ready, 2 * i + 2)
                link(g.tensor_tensor(kdecT[:, i], kgT[:, i % 2], gtmp[:, 2], ALU.mult), kdec_ready)
            pool.wait_ge(qdec_ready, 8)
            for i in range(4):
                link(g.memset(kdec[64:P, i, 0], 0.0), zeros2)
                link(g.memset(kdec[0:64, i, 1], 0.0), zeros2)
            pool.wait_ge(s_done, 1)
            for d in range(2):
                for h in range(GLA_H):
                    v = att[d][:, h].rearrange("p (t c) -> p t c", t=NT)
                    link(g.memset(v[0:64, :, 64:P], 0.0), zeros2)
                    link(g.memset(v[64:P, :, 0:64], 0.0), zeros2)

            def fetch(h):
                for t in range(NT):
                    hold(pool, topk_done, 4 * h + t + 1)
                    for s in range(TOPK):
                        n = h * GROUP + t * TOPK + s
                        b = (t * TOPK + s) % NB
                        if isinstance(h, int) and n == TOPK:
                            pool.wait_ge(y_done, NT)
                            link(g.memset(yacc[:, NT - 1], 0.0), y_zero)
                        if not isinstance(h, int) or n >= NB:
                            hold(pool, slot_summed, n - NB + 1)
                        g.indirect_dma_start(
                            ring[b], None, uv_d,
                            bass.IndirectOffsetOnAxis(ap=eidx[:, t, s:s + 1], axis=0),
                        ).then_inc(rows_in[b], 16)

            fetch(0)
            with pool.Fori(1, PH) as h:
                fetch(h)

        @block.scalar
        def _(act):
            a = nc.scalar
            tell, link = linker(act, act_step)
            act.wait_ge(c_in, 16)
            link(a.activation(cact, craw, ACT.Silu), c_act)
            for t in range(NT):
                act.wait_ge(x_in[t], 16)
                if t == 0:
                    act.wait_ge(cols_in, 16)
                link(a.activation(xn[:, t], X[:, t], ACT.Square, accum_out=ss[:, t:t + 1]))
                link(a.activation(sd[:, t:t + 1], ss[:, t:t + 1], ACT.Sqrt, scale=1.0 / D, bias=eps), ms_ready)
            for d in range(KD):
                act.wait_ge(xT_done, d + 1)
                act.wait_ge(mod1_ready, d + 1)
                tell(a.activation(h1T[:, d], ps[:, 4 + d % 4], ACT.Identity, scale=mod[:, 2 * d:2 * d + 1],
                                  bias=mod[:, 2 * d + 1:2 * d + 2]), h1_ready)
                if d >= 4:
                    if d == 4:
                        act.wait_ge(xT_done, KD)
                    for k in (2 * d - 8, 2 * d - 7):
                        act.wait_ge(h1_ready, k + 1)
                        tell(a.activation(h1hi[k], h1T[:, k], ACT.Copy), h1_hi)

            def proj_copy(i, out, **kw):
                act.wait_ge(lat_done, i + 1)
                tell(a.activation(out, ps[:, i % 4], kw.pop("func", ACT.Copy), **kw), proj_act)

            def split_weights(n):
                act.wait_ge(win_in[n % 8], 16 * (n // 8 + 1))
                if 8 <= n < 14:
                    act.wait_ge(lat_done, n - 3)
                elif 14 <= n < 17:
                    act.wait_ge(gate_chunk, n - 13)
                elif n == 17:
                    act.wait_ge(rg_done, NT)
                tell(a.activation(whi[n % 4], wring[:, n % 8], ACT.Copy), w_hi)

            split_weights(4)
            split_weights(5)
            for i in range(5):
                act.wait_ge(lat_done, i + 1)
                tell(a.activation(latsq[i], ps[:, i % 4], ACT.Square), sq_ready)
                proj_copy(i, latT[:, i], scale=cols[:, COL_GQL + i:COL_GQL + i + 1])
                if i in (1, 3, 4):
                    split_weights({1: 6, 3: 7, 4: 8}[i])
                if i == 4:
                    act.wait_ge(angles, 2)
                    tell(a.activation(cos_t, turn, ACT.Sin), tables)
                    tell(a.activation(sin_t, ang, ACT.Sin, scale=cols[:, COL_SIGN:COL_SIGN + 1]), tables)
            proj_copy(KRG, krgT)
            split_weights(9)
            for j in range(2):
                proj_copy(QG + j, qgT[:, j], scale=DK ** -0.5)
                split_weights(10 + j)
            proj_copy(KG, kgT[:, 0])
            split_weights(12)
            for j, rank in enumerate((Q_RANK, KV_RANK)):
                act.wait_ge(ss_done, j + 1)
                tell(a.activation(tmp[:, j], ps[:, 4 + j], ACT.Sqrt, scale=1.0 / rank, bias=eps), ss_read)
            proj_copy(KG + 1, kgT[:, 1])
            for n in range(13, 17):
                split_weights(n)
            for t in range(NT):
                act.wait_ge(rg_done, t + 1)
                tell(a.activation(rg[:, t], ps[:, 4 + t], ACT.Silu), rg_evac)
            split_weights(17)
            for i in range(4):
                act.wait_ge(z_read, i + 1)
                link(a.activation(soft[:, i], gate[:, i], ACT.Abs))
            for i in range(4):
                link(a.activation(soft[:, i], soft[:, i], ACT.Exp, scale=-1.0))
            for i in range(4):
                tell(a.activation(soft[:, i], soft[:, i], ACT.Ln, bias=1.0), gate_exp)
            for t in range(NT):
                act.wait_ge(vg_done, t + 1)
                tell(a.activation(vg[:, t], ps[:, 4 + t], ACT.Copy), vg_evac)
            def decays(i):
                act.wait_ge(sums_ready, 2 * i + 1)
                if i >= 1:
                    act.wait_ge(qdec_ready, 2 * i)
                    act.wait_ge(kdec_ready, 2 * i)
                tell(a.activation(gtmp[:, 0], gate[:, i], ACT.Exp, scale=1.0 / GATE_NORM), decay_dve)
                tell(a.activation(gtmp[:, 1], gate[:, i], ACT.Exp, scale=-1.0 / GATE_NORM), decay_ready)
                act.wait_ge(sums_ready, 2 * i + 2)
                tell(a.activation(gtmp[:, 2], tmp[:, i % 2], ACT.Exp, scale=1.0 / GATE_NORM), decay_ready)
                link(a.activation(edge[:, i], gate[:, i][:, (CHUNK - 1 if i < 2 else 0)::CHUNK], ACT.Exp,
                                  scale=1.0 / GATE_NORM), decay_dve)

            act.wait_ge(mods_ready, 1)
            act.wait_ge(ss_read, 2)
            for u in (0, 1, 2, 3, 4, 5, 8, 9, 10, 11, 12, 13, 14, 15):
                act.wait_ge(upq_done, u + 1)
                dst = (qn[:, u] if u < 4 else qr[:, u - 4] if u < 6 else kn[:, u - 8] if u < 12 else vm[:, u - 12])
                tell(a.activation(dst, ps[:, u % 4], ACT.Copy), up_act)
                if u in (1, 3, 8, 11):
                    decays((1, 3, 8, 11).index(u))

            scale = (NOPE + ROPE) ** -0.5
            for n in range(16 + 2):
                if n < 16:
                    act.wait_ge(max_ready, n + 1)
                    if n >= 4:
                        act.wait_ge(pt_done, n - 3)
                    tell(a.activation(prob[:, n % 4], ps[:, n % 4], ACT.Exp, scale=scale,
                                      bias=nmax[:, n:n + 1], accum_out=rsum[:, n:n + 1]), exp_done)
                m = n - 2
                if m >= 0:
                    act.wait_ge(pt_done, m + 1)
                    if m % 4 == 0 and m:
                        act.wait_ge(o_done, m // 4)
                    tell(a.activation(probT[:, :, (m % 4) * P:(m % 4 + 1) * P],
                                      ps[:, 4 + m % 2].rearrange("p (k q) -> p k q", k=NT), ACT.Copy),
                         pt_evac)
                    if m % 4 == 0 and m:
                        act.wait_ge(o_done, m // 4)
                        tell(a.activation(mixT[:, m // 4 - 1], ps[:, 6], ACT.Copy), o_evac)
                if n % 3 == 0 and 3 <= n <= 12:
                    i = n // 3 - 1
                    if i == 0:
                        act.wait_ge(zeros2, 8)
                    act.wait_ge(kd_done, i + 1)
                    tell(a.activation(kdec[0:64, i, 0], ps[0:64, 7], ACT.Copy), kd_act)
            act.wait_ge(o_done, 4)
            tell(a.activation(mixT[:, 3], ps[:, 6], ACT.Copy), o_evac)

            for u in range(8):
                act.wait_ge(bc_done, u + 1)
                tell(a.activation(bcast[:, u // 2, (u % 2) * 512:(u % 2 + 1) * 512], ps[:, 4 + u % 4],
                                  ACT.Copy), bc_evac)

            def copy_mixT(t):
                act.wait_ge(mixT_done, t + 1)
                tell(a.activation(mixT[:, 4:8, t * P:(t + 1) * P], ps[:, 4 + t].rearrange("p (h q) -> p h q", h=GLA_H),
                                  ACT.Copy, scale=cols[:, COL_GGLA:COL_GGLA + 1]), mixT_evac)

            for t in range(NT):
                act.wait_ge(og_done, t + 1)
                if t >= 2:
                    act.wait_ge(gss_ready, t - 1)
                tell(a.activation(gsq[:, t % 2], ps[:, t], ACT.Square), gsq_ready)
                act.wait_ge(gss_ready, t + 1)
                tell(a.activation(gsd[:, t], gss[:, t], ACT.Sqrt, scale=1.0 / DV, bias=eps), gsd_ready)
                if t >= 2:
                    copy_mixT(t - 2)
            def square_y(t):
                act.wait_ge(y_done, t + 1)
                b0 = 2 * (t % 2)
                link(a.activation(junk[:, 0].rearrange("p (a b) -> p a b", a=2), ps[:, b0:b0 + 2], ACT.Square,
                                  accum_out=ss[:, t:t + 1]))
                link(a.activation(sd[:, t:t + 1], ss[:, t:t + 1], ACT.Sqrt, scale=1.0 / D, bias=eps),
                     ssy_ready)

            def square_x(t):
                act.wait_ge(x1_ready, 2 * t + 2)
                link(a.activation(junk[:, 0], X[:, t], ACT.Square, accum_out=ssb[:, t:t + 1]))
                link(a.activation(sdb[:, t:t + 1], ssb[:, t:t + 1], ACT.Sqrt, scale=1.0 / D, bias=eps),
                     ssx_ready)

            def copy_h2T(t):
                act.wait_ge(h2T_done, t + 1)
                b0 = 2 if t == 3 else 4
                for j in range(2):
                    tell(a.activation(h2T[:, 4 * j:4 * j + 4, t * P:(t + 1) * P],
                                      ps[:, b0 + j].rearrange("p (d q) -> p d q", d=4), ACT.Copy), h2T_evac)

            def copy_first_query(t):
                act.wait_ge(first_query, t + 1)
                for half in range(2):
                    tell(a.activation(qT[:, half, t * P:(t + 1) * P], ps[:, 4 + half, t * P:(t + 1) * P], ACT.Copy),
                         first_evac)

            def copy_query(h, half):
                act.wait_ge(query_done, 2 * h + half + 1)
                if not isinstance(h, int) or h > 0:
                    act.wait_ge(scores_done, 4 * h)
                a.activation(qT[:, half], ps[:, 4 + half], ACT.Copy).then_inc(query_evac, 1)

            def exp_top(h, t):
                act.wait_ge(topk_done, 4 * h + t + 1)
                a.activation(etop[:, t], tops[:, t], ACT.Exp, bias=nmx[:, t:t + 1],
                             accum_out=tsum[:, t:t + 1]).then_inc(topk_exp, 1)

            def pair(h, t, q):
                n = h * GROUP + t * TOPK + 2 * q
                k = slice(2 * q, 2 * q + 2)
                act.wait_ge(dots_done, n + 2)
                a.activation(agelu[:, t, k], adot[:, t, k], ACT.Gelu).then_inc(gelu_done, 1)
                if q == 0:
                    act.wait_ge(gates_ready, 4 * h + t + 1)
                act.wait_ge(gelu_done, h * (GROUP // 2) + t * (TOPK // 2) + q + 1)
                for s in (2 * q, 2 * q + 1):
                    a.activation(wexp[:, t, s:s + 1], agelu[:, t, s:s + 1], ACT.Copy,
                                 scale=gates[:, t, s:s + 1]).then_inc(weight_done, 1)
                for s in (2 * q, 2 * q + 1):
                    m = h * GROUP + t * TOPK + s
                    act.wait_ge(weight_done, m + 1)
                    if not isinstance(h, int) or m >= 4:
                        act.wait_ge(slot_summed, m - 3)
                    a.activation(dg[:, s % 4], ident, ACT.Copy,
                                 scale=wexp[:, t, s:s + 1]).then_inc(diag_ready, 1)

            def weigh(h, more):
                for t in range(NT):
                    for q in range(TOPK // 2):
                        first = isinstance(h, int) and h == 0 and t == 0
                        if first and q == 2:
                            copy_h2T(2)
                            square_y(3)
                        if first and q == 4:
                            last_tiles()
                        pair(h, t, q)
                        if q == (7 if first else 3) and more and t < 2:
                            copy_query(h + 1, t)
                        if q == (7 if first else 3):
                            if more or t < 3:
                                exp_top(h if t < 3 else h + 1, (t + 1) % NT)
                        if not more and t > 0 and q == 4:
                            square_sums(t - 1)

            def last_tiles():
                square_x(3)
                copy_h2T(3)
                for half in range(2):
                    act.wait_ge(query_done, half + 1)
                    a.activation(qT[:, half, 2 * P:], ps[:, 4 + half, 2 * P:], ACT.Copy).then_inc(query_evac, 1)

            def square_sums(t):
                act.wait_ge(y_taken, NT * (PH - 1) + t + 1)
                link(a.activation(junk[:, 0], yacc[:, t], ACT.Square, accum_out=ss[:, t:t + 1]))
                link(a.activation(sd[:, t:t + 1], ss[:, t:t + 1], ACT.Sqrt, scale=1.0 / D, bias=eps),
                     ssf_ready)

            square_y(0)
            copy_mixT(2)
            copy_mixT(3)
            square_x(0)
            square_y(1)
            copy_h2T(0)
            square_x(1)
            copy_first_query(0)
            exp_top(0, 0)
            copy_h2T(1)
            square_y(2)
            square_x(2)
            copy_first_query(1)
            weigh(0, True)
            with act.Fori(1, PH - 1) as h:
                weigh(h, True)
            weigh(PH - 1, False)
            act.wait_ge(ssf_ready, 3)
            link(a.activation(sdb[:, 0:1], ss[:, 0:1], ACT.Sqrt, scale=1.0 / D, bias=eps))
            square_sums(3)

        @block.tensor
        def _(pe):
            mm = nc.tensor.matmul
            pe.wait_ge(const_in, 16)
            for t in range(NT):
                pe.wait_ge(xn_ready, t + 1)
                for d in range(4):
                    last = nc.tensor.transpose(ps[:, 4 + d, t * P:(t + 1) * P], xn[:, t, d * P:(d + 1) * P], ident)
                    if t == NT - 1:
                        last.then_inc(xT_done, 1)
            for k in range(KD):
                pe.wait_ge(h1_ready, k + 1)
                if k < 4:
                    for t in range(NT):
                        last = nc.tensor.transpose(ps[:, 4 + k, t * P:(t + 1) * P],
                                                   xn[:, t, (k + 4) * P:(k + 5) * P], ident)
                    last.then_inc(xT_done, 1)
                pe.wait_ge(win_in[k // 2], 16)
                w = wring[:, k // 2].rearrange("p (k m) -> p k m", k=2)
                for i in range(4):
                    last = mm(ps[:, i], w[:, k % 2, i * P:(i + 1) * P], h1T[:, k], start=(k == 0),
                              stop=(k == KD - 1), skip_group_check=True)
                    if k == KD - 1:
                        last.then_inc(lat_done, 1)
                if k < KD - 1:
                    last.then_inc(rows_used, 1)

            def parts(n, kt):
                return [w.rearrange("p (k m) -> p k m", k=kt) for w in (whi[n % 4], wlo[n % 8])]

            def proj_tile(i):
                pe.wait_ge(w_hi, i - 3)
                pe.wait_ge(proj_act, i - 3)
                hi, lo = parts(i, KD)
                for k in range(KD):
                    if i == 4:
                        pe.wait_ge(h1_hi, k + 1)
                    mm(ps[:, i % 4], hi[:, k], h1hi[k], start=(k == 0), stop=False)
                for k in range(KD):
                    if i == 4:
                        pe.wait_ge(h1_lo, k + 1)
                    mm(ps[:, i % 4], hi[:, k], h1lo[k], start=False, stop=False)
                pe.wait_ge(w_lo, i - 3)
                for k in range(KD):
                    last = mm(ps[:, i % 4], lo[:, k], h1hi[k], start=False, stop=(k == KD - 1))
                last.then_inc(lat_done, 1)

            proj_tile(4)
            proj_tile(5)
            proj_tile(6)
            pe.wait_ge(perm_in, 32)
            pe.wait_ge(proj_act, KRG + 1)
            for j, m in enumerate((dup_k, swap_k)):
                mm(ps[:, 6 + j], m[0:ROPE], krgT[0:ROPE], start=True, stop=True).then_inc(kr_done, 1)
            proj_tile(7)
            proj_tile(8)
            for j, k1 in enumerate((3, 5)):
                pe.wait_ge(sq_summed, j + 1)
                mm(ps[:, 4 + j], ones, latsq[k1 - 1], start=True, stop=True).then_inc(ss_done, 1)
            proj_tile(9)
            def project_tokens(first, done):
                for j in range(4):
                    i = first + j
                    pe.wait_ge(w_lo, i - 3)
                    hi, lo = parts(i, 2)
                    for t in range(NT):
                        for kk in range(2):
                            k, q = 2 * j + kk, slice(t * P, (t + 1) * P)
                            for n, (h, w) in enumerate(((h1hi, hi), (h1hi, lo), (h1lo, hi))):
                                last = mm(ps[:, 4 + t], h[k][:, q], w[:, kk], start=(k == 0 and n == 0),
                                          stop=(k == KD - 1 and n == 2), skip_group_check=True)
                        if j == 3:
                            last.then_inc(done, 1)
                    if j < 3 and first == IN_TILES:
                        last.then_inc(gate_chunk, 1)

            pe.wait_ge(ss_read, 2)
            pe.wait_ge(kr_read, 2)
            project_tokens(IN_TILES, rg_done)
            pe.wait_ge(proj_act, IN_TILES)
            for i in range(4):
                mm(ps[:, i], wgate[64:96, i // 2, i % 2], krgT[64:96], start=True, stop=True).then_inc(z_done, 1)
            pe.wait_ge(rg_evac, NT)
            project_tokens(IN_TILES + 4, vg_done)
            for u in range(16):
                if u == 0:
                    pe.wait_ge(up_in, 48)
                    pe.wait_ge(lat_ready, 3)
                if u == 8:
                    pe.wait_ge(lat_ready, 5)
                if u < 4:
                    pe.wait_ge(z_read, u + 1)
                else:
                    wait_unit_evacuated(pe, u - 4)
                if 6 <= u < 8:
                    wait_unit_evacuated(pe, u - 2)
                    last = mm(ps[:, u % 4], swap_q, qr[:, u - 6], start=True, stop=True)
                elif u < 6:
                    for k in range(3):
                        last = mm(ps[:, u % 4], wqup[:, k, u], latT[:, k], start=(k == 0), stop=(k == 2))
                elif u < 12:
                    for k in range(2):
                        last = mm(ps[:, u % 4], wkvup[:, k, (u - 8) * P:(u - 7) * P], latT[:, 3 + k],
                                  start=(k == 0), stop=(k == 1))
                else:
                    for k in range(2):
                        last = mm(ps[:, u % 4], latT[:, 3 + k, (u - 12) * P:(u - 11) * P], wkvup[:, k, 512:1024],
                                  start=(k == 0), stop=(k == 1))
                last.then_inc(upq_done, 1)

            def scores(n):
                h, q = n // 4, n % 4
                r = 64 * (h % 2)
                if n < 4:
                    wait_unit_evacuated(pe, 12 + n)
                else:
                    pe.wait_ge(exp_done, n - 3)
                mm(ps[:, n % 4], qn[:, h, q * P:(q + 1) * P], kn[:, h], start=True, stop=False)
                mm(ps[:, n % 4], qr[r:r + 64, h // 2, q * P:(q + 1) * P], krope[r:r + 64],
                   start=False, stop=True).then_inc(s_done, 1)

            def values(h):
                pe.wait_ge(pt_evac, 4 * h + 4)
                if h:
                    pe.wait_ge(o_evac, h)
                for k in range(NT):
                    last = mm(ps[:, 6], vm[:, k, h * P:(h + 1) * P], probT[:, k], start=(k == 0), stop=(k == 3))
                last.then_inc(o_done, 1)

            def turn_keys(i):
                pe.wait_ge(kdec_ready, 2 * i + 2)
                if i:
                    pe.wait_ge(kd_act, i)
                    pe.wait_ge(kd_dve, i)
                for t in range(NT):
                    last = nc.tensor.transpose(ps[:, 7, t * P:(t + 1) * P], kdecT[:, i, t * P:(t + 1) * P], ident)
                last.then_inc(kd_done, 1)

            pe.wait_ge(up_act, 14)
            pe.wait_ge(rope_ready, 3)
            pe.wait_ge(vg_evac, NT)
            for n in range(3):
                scores(n)
            for n in range(16):
                pe.wait_ge(prob_ready, n + 1)
                if n >= 2:
                    pe.wait_ge(pt_evac, n - 1)
                for k in range(NT):
                    last = nc.tensor.transpose(ps[:, 4 + n % 2, k * P:(k + 1) * P],
                                               prob[:, n % 4, k * P:(k + 1) * P], ident)
                last.then_inc(pt_done, 1)
                if n + 3 < 16:
                    scores(n + 3)
                if n % 3 == 0 and n < 12:
                    turn_keys(n // 3)
                if n % 4 == 0 and n:
                    values(n // 4 - 1)

            def chunk_states(i):
                d, p = i // 2, i % 2
                for c in range(7):
                    cc = c if d == 0 else 7 - c
                    for hh in range(2):
                        last = mm(ps[64 * hh:64 * hh + 64, 2 * i + c // 4, (c % 4) * DV:(c % 4 + 1) * DV],
                                  kdec[:, i, cc % 2, (cc // 2) * P + 64 * hh:(cc // 2) * P + 64 * hh + 64],
                                  vg[:, cc // 2, (2 * p + hh) * DV:(2 * p + hh + 1) * DV], start=True, stop=True)
                last.then_inc(ds_done, 1)

            def chunk_scores(d):
                pe.wait_ge(state_ready, d + 1)
                for h in range(GLA_H):
                    i = d * 2 + h // 2
                    n = d * GLA_H + h
                    for t in range(NT):
                        for par in range(2):
                            k0 = t * P + par * 64
                            last = mm(ps[par * 64:par * 64 + 64, n // 2,
                                         (n % 2) * 256 + t * 64:(n % 2) * 256 + t * 64 + 64],
                                      kinv[:, i, k0:k0 + 64], qdec[:, d, h, k0:k0 + 64], start=True, stop=True)
                    last.then_inc(att_done, 1)

            pe.wait_ge(zeros2, 8)
            pe.wait_ge(kd_act, 4)
            pe.wait_ge(kd_dve, 4)
            pe.wait_ge(exp_done, 16)
            chunk_states(0)
            chunk_states(1)
            values(3)
            pe.wait_ge(zeros_ready, 8)
            pe.wait_ge(qdec_ready, 8)
            chunk_scores(0)
            pe.wait_ge(o_evac, 4)
            chunk_states(2)
            chunk_states(3)
            chunk_scores(1)
            pe.wait_ge(state_ready, 4)
            for u in range(8):
                pe.wait_ge(diag_cols, u + 1)
                if u >= 4:
                    pe.wait_ge(bc_evac, u - 3)
                mm(ps[:, 4 + u % 4], ones, col_diag[:, u % 4], start=True, stop=True).then_inc(bc_done, 1)

            def gla_output(t):
                for h in range(GLA_H):
                    out = ps[:, t, h * P:(h + 1) * P]
                    mm(out, att[0][:, h, t * P:(t + 1) * P], vg[:, t, h * P:(h + 1) * P], start=True, stop=False,
                       skip_group_check=True)
                    for d in range(2):
                        for par in range(2):
                            c = 2 * t + par
                            k = c if d == 0 else 7 - c
                            if k == 0:
                                continue
                            off = (k - 1) * DV
                            mm(out[par * 64:par * 64 + 64], qdec[:, d, h, c * 64:c * 64 + 64],
                               state[:, d * 2 + h // 2, off:off + DV], start=False, stop=False,
                               skip_group_check=True)
                    last = mm(out, att[1][:, h, t * P:(t + 1) * P], vg[:, t, h * P:(h + 1) * P], start=False,
                              stop=True, skip_group_check=True)
                last.then_inc(og_done, 1)

            def transpose_mix(t):
                pe.wait_ge(mix_ready, t + 1)
                for h in range(GLA_H):
                    last = nc.tensor.transpose(ps[:, 4 + t, h * P:(h + 1) * P], gmix[:, t % 2, h * P:(h + 1) * P], ident)
                last.then_inc(mixT_done, 1)

            pe.wait_ge(zeros2, 24)
            pe.wait_ge(att_ready, 8)
            gla_output(0)
            gla_output(1)
            gla_output(2)
            pe.wait_ge(bc_evac, 8)
            transpose_mix(0)
            gla_output(3)
            transpose_mix(1)
            pe.wait_ge(wout_in, 16)

            def project_out(t, between=()):
                b0 = 2 * (t % 2)
                pe.wait_ge(mixT_evac, t + 1)
                if t >= 2:
                    pe.wait_ge(x1_ready, 2 * (t - 2) + 1)
                if t == 1:
                    pe.wait_ge(mix_ready, NT)
                for half in range(2):
                    if half == 1:
                        for step, tile in between:
                            step(tile)
                    for k in range(KD):
                        last = mm(ps[:, b0 + half], mixT[:, k, t * P:(t + 1) * P],
                                  wout[:, k, half * 512:(half + 1) * 512], start=(k == 0), stop=(k == KD - 1))
                last.then_inc(y_done, 1)

            def transpose_h2(t):
                pe.wait_ge(h2_ready, t + 1)
                if t == 0:
                    pe.wait_ge(mixT_evac, NT)
                else:
                    pe.wait_ge(first_evac, 2 * min(t, 2))
                b0 = 2 if t == 3 else 4
                for d in range(KD):
                    last = nc.tensor.transpose(ps[:, b0 + d // 4, (d % 4) * P:(d % 4 + 1) * P],
                                               h2[:, t, d * P:(d + 1) * P], ident)
                last.then_inc(h2T_done, 1)

            def first_head(t0, t1):
                pe.wait_ge(h2T_evac, 2 * t1)
                for half in range(2):
                    for k in range(KD):
                        last = mm(ps[:, 4 + half, t0 * P:t1 * P], wpq[:, k, half * P:(half + 1) * P],
                                  h2T[:, k, t0 * P:t1 * P], start=(k == 0), stop=(k == KD - 1))
                    if t0 == 2:
                        last.then_inc(query_done, 1)
                if t0 < 2:
                    last.then_inc(first_query, 1)
                    pe.wait_ge(first_evac, 2 * t1)
                    if t0 == 1:
                        pe.wait_ge(topk_done, 1)
                    tile_scores(t0)
                else:
                    pe.wait_ge(query_evac, 2)
                    tile_scores(2)
                    tile_scores(3)

            def tile_scores(t):
                for half in range(2):
                    c0 = (t % 2) * 256 + half * P
                    last = mm(ps[:, 6 + t // 2, c0:c0 + P], qT[:, half, t * P:(t + 1) * P], keys[:, half],
                              start=True, stop=True)
                last.then_inc(scores_done, 1)

            def query(h, half):
                if half == 0:
                    pe.wait_ge(wpq_in, 16 * h + 16)
                if not isinstance(h, int) or h > 0:
                    pe.wait_ge(query_evac, 2 * h - 1 + half)
                for k in range(KD):
                    last = mm(ps[:, 4 + half], wpq[:, k, half * P:(half + 1) * P], h2T[:, k],
                              start=(k == 0), stop=(k == KD - 1))
                last.then_inc(query_done, 1)

            def key_scores(h):
                pe.wait_ge(query_evac, 2 * h + 2)
                if not isinstance(h, int) or h > 0:
                    pe.wait_ge(topk_done, 4 * h)
                for t in range(NT):
                    tile_scores(t)

            def expert_sums(h, t, s0=0, s1=TOPK):
                for s in range(s0, s1):
                    n = h * GROUP + t * TOPK + s
                    pe.wait_ge(diag_ready, n + 1)
                    if s == 0 and (not isinstance(h, int) or 4 * h + t >= 2):
                        pe.wait_ge(y_taken, 4 * h + t - 1)
                    for half in range(2):
                        last = mm(ps[:, 2 * (t % 2) + half], dg[:, s % 4],
                                  ring[(t * TOPK + s) % NB][:, D + half * 512:D + (half + 1) * 512],
                                  start=(s == 0), stop=(s == TOPK - 1))
                    last.then_inc(slot_summed, 1)

            def expert_head(h, more):
                if more:
                    query(h + 1, 0)
                expert_sums(h, 0)
                if more:
                    query(h + 1, 1)
                expert_sums(h, 1)
                if more:
                    key_scores(h + 1)
                expert_sums(h, 2)
                expert_sums(h, 3)

            project_out(0)
            project_out(1, [(transpose_mix, 2), (transpose_mix, 3)])
            transpose_h2(0)
            pe.wait_ge(wpq_in, 16)
            first_head(0, 1)
            project_out(2, [(transpose_h2, 1)])
            first_head(1, 2)
            project_out(3, [(transpose_h2, 2)])
            pe.wait_ge(x1_ready, 5)
            expert_sums(0, 0, 0, TOPK // 2)
            transpose_h2(3)
            first_head(2, 4)
            expert_sums(0, 0, TOPK // 2, TOPK)
            query(1, 0)
            query(1, 1)
            expert_sums(0, 1)
            key_scores(1)
            expert_sums(0, 2)
            expert_sums(0, 3)
            with pe.Fori(1, PH - 1) as h:
                expert_head(h, True)
            expert_head(PH - 1, False)

        @block.vector
        def _(dve):
            v = nc.vector
            tell, link = linker(dve, dve_step)
            def reduce_mods(n0, n1):
                for n in range(n0, n1):
                    if n < 8:
                        dve.wait_ge(ada_in[n % 4], 16 * (n // 4 + 1))
                    else:
                        dve.wait_ge(ada_late[n % 4], 16 * (n // 4 - 1))
                    for j in range(2):
                        m = 2 * n + j
                        tell(v.tensor_tensor_reduce(out=ada[:, n % 4, j], in0=ada[:, n % 4, j], in1=cact,
                                                    scale=1.0, scalar=0.0, op0=ALU.mult, op1=ALU.add,
                                                    accum_out=mod[:, m:m + 1]), ada_used)

            def normalise(t):
                dve.wait_ge(ms_ready, t + 1)
                link(v.reciprocal(rstd[:, t:t + 1], sd[:, t:t + 1]))
                tell(v.tensor_scalar(xn[:, t], X[:, t], rstd[:, t:t + 1], None, ALU.mult), xn_ready)

            def first_mods(k):
                reduce_mods(k, k + 1)
                dve.wait_ge(ada_used, 2 * k + 2)
                link(v.tensor_tensor(mod[:, 2 * k:2 * k + 2], mod[:, 2 * k:2 * k + 2], cols[:, 2 * k:2 * k + 2], ALU.add))
                link(v.scalar_tensor_tensor(out=mod[:, 2 * k:2 * k + 1], in0=mod[:, 2 * k:2 * k + 1], scalar=1.0,
                                            in1=cols[:, COL_GPM + k:COL_GPM + k + 1], op0=ALU.add, op1=ALU.mult),
                     mod1_ready)

            dve.wait_ge(c_act, 1)
            dve.wait_ge(cols_in, 16)
            dve.wait_ge(const_in, 16)
            for t in range(3):
                normalise(t)
            first_mods(0)
            normalise(3)
            for k in range(1, KD):
                first_mods(k)
            for k in range(KD):
                dve.wait_ge(h1_hi, k + 1)
                if k < KD - 1:
                    dve.wait_ge(rows_used, k + 1)
                else:
                    dve.wait_ge(lat_done, 4)
                tell(v.tensor_tensor(h1lo[k], h1T[:, k], h1hi[k].bitcast(f32), ALU.subtract), h1_lo)
            dve.wait_ge(pos_in, 16)
            link(v.tensor_copy(ang, pos_i.bitcast(i32)))
            link(v.tensor_scalar(ang, ang, cols[:, COL_INV:COL_INV + 1], None, ALU.mult))
            red = turned[:, 0]
            for k, (buf, quarter) in enumerate(((turn, 0.25), (ang, 0.0))):
                link(v.tensor_scalar(red, ang, 1.0 / TWO_PI, quarter, ALU.mult, ALU.add))
                link(v.tensor_scalar(red, red, ROUND, ROUND, ALU.add, ALU.subtract))
                src = ang
                for part in (PI_A, PI_B, PI_C):
                    link(v.scalar_tensor_tensor(out=buf, in0=red, scalar=-part, in1=src, op0=ALU.mult, op1=ALU.add))
                    src = buf
                link(v.tensor_scalar(buf, buf, HALF_PI if k == 0 else 0.0, PI_MAX, ALU.add, ALU.min))
                link(v.tensor_scalar(buf, buf, -PI_MAX, None, ALU.max), angles)
            reduce_mods(8, 12)

            def rotate(out, straight, swapped, read):
                link(v.tensor_tensor(turned[:, 0], straight, cos_t, ALU.mult), read)
                link(v.tensor_tensor(turned[:, 1], swapped, sin_t, ALU.mult), read)
                link(v.tensor_tensor(out, turned[:, 0], turned[:, 1], ALU.add), rope_ready)

            for k, k1 in ((1, 3), (2, 3), (4, 5)):
                dve.wait_ge(sq_ready, k + 1)
                link(v.tensor_tensor(latsq[k], latsq[k], latsq[k - 1], ALU.add),
                     sq_summed if k + 1 == k1 else dve_step)
            dve.wait_ge(tables, 2)
            dve.wait_ge(kr_done, 2)
            rotate(krope, ps[:, 6], ps[:, 7], kr_read)
            reduce_mods(12, 16)
            for j, (k0, k1) in enumerate(((0, 3), (3, 5))):
                dve.wait_ge(ss_read, j + 1)
                link(v.reciprocal(tmp[:, j], tmp[:, j]))
                for k in range(k0, k1):
                    dve.wait_ge(proj_act, k + 1)
                    tell(v.tensor_tensor(latT[:, k], latT[:, k], tmp[:, j], ALU.mult), lat_ready)
            reduce_mods(16, 24)
            dve.wait_ge(ada_used, N_MOD)
            rest = slice(2 * KD, N_MOD)
            link(v.tensor_tensor(mod[:, rest], mod[:, rest], cols[:, rest], ALU.add))
            link(v.tensor_tensor(mod[:, GT1:GT1 + KD], mod[:, GT1:GT1 + KD], cols[:, COL_GQM:COL_GQM + KD], ALU.mult))
            link(v.scalar_tensor_tensor(out=mod[:, SC2:SC2 + KD], in0=mod[:, SC2:SC2 + KD], scalar=1.0,
                                        in1=cols[:, COL_GPF:COL_GPF + KD], op0=ALU.add, op1=ALU.mult))
            link(v.tensor_tensor(mod[:, GT2:GT2 + KD], mod[:, GT2:GT2 + KD], cols[:, COL_GQF:COL_GQF + KD], ALU.mult),
                 mods_ready)
            for i in range(4):
                dve.wait_ge(z_done, i + 1)
                tell(v.tensor_scalar(gate[:, i], ps[:, i], cols[:, COL_BG + i:COL_BG + i + 1], None, ALU.add),
                     z_read)
            for i in range(4):
                dve.wait_ge(gate_exp, i + 1)
                link(v.scalar_tensor_tensor(out=gate[:, i], in0=gate[:, i], scalar=0.0, in1=soft[:, i],
                                            op0=ALU.min, op1=ALU.subtract))

            def running_sums(i):
                g_i = gate[:, i] if i < 2 else gate[:, i][:, ::-1]
                link(v.tensor_tensor_scan(g_i, scan_keep, g_i, 0.0, ALU.mult, ALU.add), sums_ready)
                if i >= 2:
                    dve.wait_ge(decay_ready, 2 * (i - 1))
                gc = gate[:, i].rearrange("p (c j) -> p c j", c=NCH)
                at_end = CHUNK - 1 if i < 2 else 0
                link(v.tensor_tensor(tmp[:, i % 2].rearrange("p (c j) -> p c j", c=NCH),
                                     gc[:, :, at_end:at_end + 1].to_broadcast([P, NCH, CHUNK]), gc, ALU.subtract),
                     sums_ready)

            def decayed_queries(i):
                dve.wait_ge(decay_dve, 2 * i + 2)
                for hh in range(2):
                    rows = slice(64 * hh, 64 * hh + 64)
                    tell(v.tensor_tensor(qdec[rows, i // 2, 2 * (i % 2) + hh], qgT[rows, i % 2], gtmp[rows, 0],
                                         ALU.mult), qdec_ready)

            running_sums(0)
            running_sums(1)
            dve.wait_ge(vg_done, NT)
            dve.wait_ge(proj_act, IN_TILES)
            decayed_queries(0)
            running_sums(2)
            decayed_queries(1)
            running_sums(3)
            for pair in range(2):
                dve.wait_ge(upq_done, 7 + pair)
                rotate(qr[:, pair], qr[:, pair], ps[:, 2 + pair], up_dve)
            decayed_queries(2)
            decayed_queries(3)
            scale = (NOPE + ROPE) ** -0.5
            for n in range(16 + 2):
                if n < 16:
                    dve.wait_ge(s_done, n + 1)
                    link(v.reduce_max(smax[:, n:n + 1], ps[:, n % 4], AX.X))
                    link(v.tensor_scalar(nmax[:, n:n + 1], smax[:, n:n + 1], -scale, None, ALU.mult), max_ready)
                m = n - 1
                if 0 <= m < 16:
                    dve.wait_ge(exp_done, m + 1)
                    link(v.reciprocal(rinv[:, m:m + 1], rsum[:, m:m + 1]))
                    tell(v.tensor_scalar(prob[:, m % 4], prob[:, m % 4], rinv[:, m:m + 1], None, ALU.mult),
                         prob_ready)
                if n % 3 == 0 and 3 <= n <= 12:
                    i = n // 3 - 1
                    if i == 0:
                        dve.wait_ge(zeros2, 8)
                    dve.wait_ge(kd_done, i + 1)
                    tell(v.tensor_copy(kdec[64:P, i, 1], ps[64:P, 7]), kd_dve)

            def on_diagonals(u):
                m = (GT1, SC2, SH2, GT2)[u // 2] + 4 * (u % 2)
                tell(v.tensor_tensor(col_diag[:, u % 4].rearrange("p (k j) -> p k j", k=4),
                                     ident.unsqueeze(1).to_broadcast([P, 4, P]),
                                     mod[:, m:m + 4].unsqueeze(2).to_broadcast([P, 4, P]), ALU.mult), diag_cols)

            for u in range(4):
                on_diagonals(u)
            def mask_scores(d):
                dve.wait_ge(zeros2, 24)
                for p in range(2):
                    dve.wait_ge(att_done, d * GLA_H + 2 * p + 2)
                    for par in range(2):
                        rows = slice(64 * par, 64 * par + 64)
                        tell(v.tensor_tensor(
                            att[d][rows, 2 * p:2 * p + 2].rearrange("p h (t c) -> p (h t) c", t=NT)
                            [:, :, 64 * par:64 * par + 64],
                            ps[rows, d * 2 + p].rearrange("p (t c) -> p t c", t=2 * NT),
                            tri[rows, d:d + 1, :].to_broadcast([64, 2 * NT, CHUNK]), ALU.mult), att_ready)

            for i in range(4):
                dve.wait_ge(ds_done, i + 1)
                for c in range(7):
                    add = ps[:, 2 * i + c // 4, (c % 4) * DV:(c % 4 + 1) * DV]
                    cur = state[:, i, c * DV:(c + 1) * DV]
                    if c == 0:
                        link(v.tensor_copy(cur, add))
                    else:
                        cc = c if i < 2 else 7 - c
                        link(v.scalar_tensor_tensor(out=cur, in0=state[:, i, (c - 1) * DV:c * DV],
                                                    scalar=edge[:, i, cc:cc + 1], in1=add,
                                                    op0=ALU.mult, op1=ALU.add),
                             state_ready if c == 6 else dve_step)
                if i == 1:
                    mask_scores(0)
            mask_scores(1)
            for u in range(4, 8):
                dve.wait_ge(bc_done, u - 3)
                on_diagonals(u)
            for t in range(NT):
                og = ps[:, t].rearrange("p (h v) -> p h v", h=GLA_H)
                mix = gmix[:, t % 2].rearrange("p (h v) -> p h v", h=GLA_H)
                dve.wait_ge(gsq_ready, t + 1)
                link(v.tensor_reduce(gss[:, t], gsq[:, t % 2].rearrange("p (h v) -> p h v", h=GLA_H), AX.X, ALU.add),
                     gss_ready)
                dve.wait_ge(gsd_ready, t + 1)
                link(v.reciprocal(grstd[:, t], gsd[:, t]))
                if t >= 2:
                    dve.wait_ge(mixT_done, t - 1)
                link(v.tensor_tensor(mix, og, grstd[:, t].unsqueeze(2).to_broadcast([P, GLA_H, DV]), ALU.mult))
                link(v.tensor_tensor(gmix[:, t % 2], gmix[:, t % 2], rg[:, t], ALU.mult), mix_ready)
            dve.wait_ge(bc_evac, 8)

            def norm_y(t):
                b0 = 2 * (t % 2)
                dve.wait_ge(ssy_ready, t + 1)
                link(v.reciprocal(rstd[:, t:t + 1], sd[:, t:t + 1]))
                link(v.scalar_tensor_tensor(out=h2[:, t].rearrange("p (a b) -> p a b", a=2),
                                            in0=ps[:, b0:b0 + 2], scalar=rstd[:, t:t + 1],
                                            in1=bcast[:, 0].rearrange("p (a b) -> p a b", a=2),
                                            op0=ALU.mult, op1=ALU.mult), x1_ready)
                link(v.tensor_tensor(X[:, t], X[:, t], h2[:, t], ALU.add), x1_ready)

            def norm_x(t):
                dve.wait_ge(ssx_ready, t + 1)
                link(v.reciprocal(rstdb[:, t:t + 1], sdb[:, t:t + 1]))
                link(v.scalar_tensor_tensor(out=h2[:, t], in0=X[:, t], scalar=rstdb[:, t:t + 1], in1=bcast[:, 1],
                                            op0=ALU.mult, op1=ALU.mult))
                link(v.tensor_tensor(h2[:, t], h2[:, t], bcast[:, 2], ALU.add), h2_ready)

            STAGES = 13

            def topk_stage(h, t, k):
                step = [2 * k]

                def link(ins, alone=False):
                    step[0] += 1
                    ins.then_inc(topk_step, 1)
                    value = (4 * h + t) * (2 * STAGES - 1) + step[0]
                    if alone:
                        hold(dve, topk_step, value)
                    else:
                        dve.wait_ge(topk_step, value)

                s = [ps[:, 6 + t // 2, (t % 2) * 256 + j * P:(t % 2) * 256 + (j + 1) * P] for j in range(2)]
                lo, hi = slice(0, 8), slice(8, 16)
                cand3 = cand.rearrange("p (a b) -> p a b", a=TOPK)
                oh = onehot.rearrange("p a k j -> p (a k) j")
                if k == 0:
                    alone = isinstance(h, int) and h == 0 and t < 2
                    hold(dve, scores_done, 4 * h + (t if alone else t | 1) + 1)
                    link(v.max(v12[:, 0, lo], s[0]), True)
                    link(v.max(v12[:, 1, lo], s[1]), True)
                elif k == 1:
                    link(v.max_index(i12[:, 0, lo], v12[:, 0, lo], s[0]), True)
                    link(v.max_index(i12[:, 1, lo], v12[:, 1, lo], s[1]), True)
                elif k == 2:
                    link(v.match_replace(srest[:, 0], v12[:, 0, lo], s[0], NEG), True)
                    link(v.match_replace(srest[:, 1], v12[:, 1, lo], s[1], NEG), True)
                elif k == 3:
                    link(v.max(v12[:, 0, hi], srest[:, 0]), True)
                    link(v.max(v12[:, 1, hi], srest[:, 1]), True)
                elif k == 4:
                    link(v.max_index(i12[:, 0, hi], v12[:, 0, hi], srest[:, 0]), True)
                    link(v.max_index(i12[:, 1, hi], v12[:, 1, hi], srest[:, 1]))
                elif k == 5:
                    link(v.tensor_tensor(cand3, v12[:, 0].unsqueeze(2).to_broadcast([P, TOPK, TOPK]),
                                         v12[:, 1:2].to_broadcast([P, TOPK, TOPK]), ALU.add), True)
                    link(v.max(tops[:, t, lo], cand), True)
                elif k == 6:
                    link(v.max_index(posn[:, lo], tops[:, t, lo], cand), True)
                    link(v.match_replace(crest, tops[:, t, lo], cand, NEG), True)
                elif k == 7:
                    link(v.max(tops[:, t, hi], crest), True)
                    link(v.max_index(posn[:, hi], tops[:, t, hi], crest))
                elif k == 8:
                    link(v.tensor_single_scalar(pab[:, 0], posn, 4, ALU.logical_shift_right))
                    link(v.tensor_single_scalar(pab[:, 1], posn, 15, ALU.bitwise_and))
                elif k == 9:
                    link(v.tensor_copy(pabf, pab))
                    link(v.tensor_copy(i12f, i12))
                elif k == 10:
                    link(v.tensor_tensor(oh, pabf.rearrange("p a k -> p (a k)").unsqueeze(2).to_broadcast([P, 32, TOPK]),
                                         iota.unsqueeze(1).to_broadcast([P, 32, TOPK]), ALU.is_equal))
                    link(v.tensor_tensor(onehot[:, 0], onehot[:, 0], i12f[:, 0:1].to_broadcast([P, TOPK, TOPK]),
                                         ALU.mult))
                elif k == 11:
                    link(v.tensor_tensor(onehot[:, 1], onehot[:, 1], i12f[:, 1:2].to_broadcast([P, TOPK, TOPK]),
                                         ALU.mult))
                    link(v.tensor_reduce(sel.rearrange("p a k -> p (a k)"), oh, AX.X, ALU.add))
                else:
                    link(v.scalar_tensor_tensor(out=eidx[:, t], in0=sel[:, 0], scalar=float(NKEYS), in1=sel[:, 1],
                                                op0=ALU.mult, op1=ALU.add))
                    v.tensor_scalar(nmx[:, t:t + 1], tops[:, t, 0:1], -1.0, None, ALU.mult).then_inc(topk_done, 1)

            def finish_gates(h, t):
                dve.wait_ge(topk_exp, 4 * h + t + 1)
                v.reciprocal(tinv[:, t:t + 1], tsum[:, t:t + 1]).then_inc(tinv_done, 1)
                dve.wait_ge(tinv_done, 4 * h + t + 1)
                v.tensor_scalar(gates[:, t], etop[:, t], tinv[:, t:t + 1], None, ALU.mult).then_inc(gates_ready, 1)

            def take_sums(h, t):
                dve.wait_ge(slot_summed, h * GROUP + (t + 1) * TOPK)
                if not isinstance(h, int) or h > 0:
                    dve.wait_ge(y_taken, 4 * h + t)
                y = yacc[:, t].rearrange("p (a b) -> p a b", a=2)
                sums = ps[:, 2 * (t % 2):2 * (t % 2) + 2]
                if isinstance(h, int) and h == 0 and t < NT - 1:
                    v.tensor_copy(y, sums).then_inc(y_taken, 1)
                else:
                    v.tensor_tensor(y, y, sums, ALU.add).then_inc(y_taken, 1)

            def dot(h, t, s):
                b = (t * TOPK + s) % NB
                dve.wait_ge(rows_in[b], 16 * (h * (GROUP // NB) + (t * TOPK + s) // NB + 1))
                v.tensor_tensor_reduce(out=ring[b][:, 0:D], in0=ring[b][:, 0:D], in1=h2[:, t], scale=1.0,
                                       scalar=0.0, op0=ALU.mult, op1=ALU.add,
                                       accum_out=adot[:, t, s:s + 1]).then_inc(dots_done, 1)

            def score_experts(h, more, tiles=range(NT)):
                for t in tiles:
                    ahead = (h, t + 2) if t < 2 else (h + 1, t - 2)
                    following = (h, t + 1) if t < 3 else (h + 1, 0)
                    for s in range(TOPK):
                        dot(h, t, s)
                        if s >= TOPK - STAGES and (more or t < 2):
                            topk_stage(*ahead, s - (TOPK - STAGES))
                        if s == 4 and t > 0:
                            take_sums(h, t - 1)
                        if s == 4 and t == 0:
                            take_sums(h - 1, NT - 1)
                        if s == 11 and (more or t < 3):
                            finish_gates(*following)
                        if s == 14 and not more and t > 0:
                            finish(t - 1)

            def finish(t):
                dve.wait_ge(ssf_ready, t + 1)
                link(v.reciprocal(rstd[:, t:t + 1], sd[:, t:t + 1]))
                link(v.scalar_tensor_tensor(out=fout[:, t], in0=yacc[:, t], scalar=rstd[:, t:t + 1], in1=bcast[:, 3],
                                            op0=ALU.mult, op1=ALU.mult))
                link(v.tensor_tensor(fout[:, t], fout[:, t], X[:, t], ALU.add), out_ready)

            for t in range(2):
                norm_y(t)
                norm_x(t)
            for k in range(STAGES):
                topk_stage(0, 0, k)
            norm_y(2)
            norm_x(2)
            finish_gates(0, 0)
            for s in range(3):
                dot(0, 0, s)
            for k in range(STAGES):
                topk_stage(0, 1, k)
            for s in range(3, 6):
                dot(0, 0, s)
            norm_y(3)
            for s in range(6, 8):
                dot(0, 0, s)
            norm_x(3)
            for s in range(8, TOPK):
                dot(0, 0, s)
            for k in range(STAGES):
                topk_stage(0, 2, k)
            finish_gates(0, 1)
            dve.wait_ge(y_zero, 1)
            score_experts(0, True, range(1, NT))
            with dve.Fori(1, PH - 1) as h:
                score_experts(h, True)
            score_experts(PH - 1, False)
            take_sums(PH - 1, NT - 1)
            finish(3)


def kernel(x, c, positions, w_ada, b_ada, g_pre_mix, g_post_mix, w_in, g_q_latent, w_q_up,
           g_kv_latent, w_kv_up, w_gate_fwd, b_gate_fwd, w_gate_bwd, b_gate_bwd, g_gla_norm,
           w_out, g_pre_ffn, g_post_ffn, w_peer_q, sub_keys_1, sub_keys_2, expert_u, expert_v):
    import numpy as np
    import concourse.bacc as bacc
    from concourse import mybir as mb
    from concourse.bass_utils import run_bass_kernel_spmd

    f = np.float32

    def feature_cols(vec):
        return np.asarray(vec).reshape(-1, P).T

    def k_major(w, n):
        return np.asarray(w).reshape(-1, P, w.shape[-1]).transpose(1, 0, 2)

    p = np.arange(P)
    inv = np.float64(THETA) ** (-(p % 32) / 32.0)
    sign = np.where(p % 64 < 32, -1.0, 1.0)
    own = np.stack([inv, sign, np.full(P, EPS)], 1).astype(f)
    j, i = (p % 64)[:, None], np.arange(CHUNK)[None]
    const = np.concatenate([np.eye(P), np.ones((P, P)), j <= i, j >= i,
                            np.broadcast_to(np.arange(SEQ) % CHUNK != 0, (P, SEQ)),
                            np.broadcast_to(np.arange(TOPK), (P, TOPK))], 1).astype(f)

    b6 = np.asarray(b_ada)[0].reshape(6, D)
    mods = [feature_cols(b6[m]) for m in MOD_ORDER]
    cols = np.concatenate([np.stack(mods[:2], 2).reshape(P, 2 * KD)] + mods[2:]
                          + [feature_cols(g[0]) for g in (g_pre_mix, g_post_mix, g_pre_ffn, g_post_ffn)]
                          + [feature_cols(g_q_latent[0]), feature_cols(g_kv_latent[0]),
                             feature_cols(b_gate_fwd[0]), feature_cols(b_gate_bwd[0]),
                             feature_cols(g_gla_norm[0]), own], 1)
    ada = np.asarray(w_ada)[0].reshape(D, 6, KD, P)[:, list(MOD_ORDER)]
    ada = np.concatenate([ada[:, :2].transpose(0, 2, 1, 3).reshape(D, 2 * KD, P),
                          ada[:, 2:].reshape(D, 4 * KD, P)], 1)
    ada = ada.reshape(D, 24, 2, P).transpose(3, 1, 2, 0)

    w = np.asarray(w_in)[0]
    sizes = (Q_RANK, KV_RANK, ROPE, GLA_H * DK, GLA_H * DK, GLA_H * DV, GATE_RANK, GATE_RANK, GLA_H * DV)
    at = np.concatenate([[0], np.cumsum(sizes)])
    cq, ckv, kr, qg, kg, vg, gf, gb, r = (w[:, at[n]:at[n + 1]] for n in range(9))
    pad = np.zeros((D, P - ROPE - 2 * GATE_RANK), f)
    tiles = np.concatenate([cq, ckv, kr, gf, gb, pad, qg, kg], 1)
    first, gate, vals = (m.reshape(4, 2, P, 512).transpose(2, 0, 1, 3).reshape(P, 4, 1024)
                         for m in (tiles[:, :4 * P], r, vg))
    tiles = tiles.reshape(KD, P, IN_TILES, P).transpose(1, 2, 0, 3).reshape(P, IN_TILES, KD * P)
    win = np.concatenate([first, tiles[:, 4:], gate, vals], 1)
    a, b = np.arange(P)[:, None], np.arange(P)[None]
    other = b - b % 64 + (b + 32) % 64
    perm = np.concatenate([a == other, a == b % 64, a == (b + 32) % 64], 1).astype(f)

    wq = np.asarray(w_q_up)[0].reshape(Q_RANK, MLA_H, NOPE + ROPE)
    nope, rp = wq[:, :, :NOPE], wq[:, :, NOPE:]
    units = [nope[:, h] for h in range(4)] + [rp[:, 2 * k:2 * k + 2].reshape(Q_RANK, P) for k in range(2)]
    wqup = np.stack(units, 1).reshape(3, P, 6, P).transpose(1, 0, 2, 3)
    wkv = np.asarray(w_kv_up)[0].reshape(KV_RANK, MLA_H, NOPE + DV)
    wkv = np.concatenate([wkv[:, :, :NOPE].reshape(KV_RANK, 512), wkv[:, :, NOPE:].reshape(KV_RANK, 512)], 1)
    wkvup = k_major(wkv, 1024)
    wgate = np.zeros((2 * GATE_RANK, 2, 2, P), f)
    wgate[:GATE_RANK, 0] = np.asarray(w_gate_fwd)[0].reshape(GATE_RANK, 2, P)
    wgate[GATE_RANK:, 1] = np.asarray(w_gate_bwd)[0].reshape(GATE_RANK, 2, P)
    wpq = np.asarray(w_peer_q)[0].reshape(KD, P, PH, DKEY).transpose(2, 1, 0, 3)
    keys = np.stack([np.asarray(sub_keys_1)[0].T, np.asarray(sub_keys_2)[0].T], 1)
    uv = np.concatenate([np.asarray(expert_u)[0], np.asarray(expert_v)[0]], 1)

    ins = dict(x=np.asarray(x)[0], c=np.asarray(c)[0], pos=np.asarray(positions)[0], ada=ada, cols=cols,
               const=const, keys=keys, win=win, perm=perm, wqup=wqup, wkvup=wkvup, wgate=wgate,
               wout=k_major(np.asarray(w_out)[0], D), wpq=wpq, uv=uv)
    ins = {k: np.ascontiguousarray(a) for k, a in ins.items()}
    nc = bacc.Bacc("TRN2", target_bir_lowering=False, num_devices=1)
    aps = [nc.dram_tensor(f"in_{k}", a.shape, mb.dt.from_np(a.dtype), kind="ExternalInput").ap()
           for k, a in ins.items()]
    out = nc.dram_tensor("out_y", (SEQ, D), mb.dt.float32, kind="ExternalOutput").ap()
    build(nc, *aps, out)
    r = run_bass_kernel_spmd(nc, [{f"in_{k}": a for k, a in ins.items()}], core_ids=[0])
    return r.results[0]["out_y"].reshape(1, SEQ, D)
```
